# Optimizing a Trainium2 kernel written in Bass

```python
import jax, jax.numpy as jnp
from jax import lax
import numpy as np
import math

D_MODEL = 1024
BATCH = 1
SEQ = 256
DEPTH = 2

N_MIXERS = 2
N_A = (DEPTH + 1) // 2
N_B = DEPTH // 2
EPS = 1e-6

M_HEADS = 8
M_DV = D_MODEL // M_HEADS
M_DK = M_DV // 2
M_CHUNK = 128
GATE_CAP = 15.0
A_IN = 2 * M_HEADS * M_DK + 2 * D_MODEL + 2 * M_HEADS

G_CHUNK = 128
G_FFN = 4 * D_MODEL
G_HALF = G_FFN // 2
G_GROUP = 128
G_GROUPS = G_HALF // G_GROUP

FFN_HIDDEN = 4 * D_MODEL


def rmsnorm(x, g):
    xf = x.astype(jnp.float32)
    y = xf * lax.rsqrt(jnp.mean(xf * xf, axis=-1, keepdims=True) + EPS) * g.astype(jnp.float32)
    return y.astype(x.dtype)

def layernorm(x, g, b):
    xf = x.astype(jnp.float32)
    mu = jnp.mean(xf, axis=-1, keepdims=True)
    var = jnp.mean(jnp.square(xf - mu), axis=-1, keepdims=True)
    y = (xf - mu) * lax.rsqrt(var + EPS) * g.astype(jnp.float32) + b.astype(jnp.float32)
    return y.astype(x.dtype)

def _to_chunks(t, nc, d):
    bsz = t.shape[0]
    return t.reshape(bsz, nc, M_CHUNK, M_HEADS, d).transpose(0, 3, 1, 2, 4).astype(jnp.float32)

def mlstm_mixer(h, w_in, b_if, hnorm_g, w_out):
    bsz, s, _ = h.shape
    nc = s // M_CHUNK
    hk = M_HEADS * M_DK
    p = h @ w_in
    q, k, v, o, ig, fg = jnp.split(
        p, [hk, 2 * hk, 2 * hk + D_MODEL, 2 * hk + 2 * D_MODEL, 2 * hk + 2 * D_MODEL + M_HEADS], axis=-1)
    q = _to_chunks(q, nc, M_DK)
    k = _to_chunks(k, nc, M_DK) * (M_DK ** -0.5)
    v = _to_chunks(v, nc, M_DV)
    b_if = b_if.astype(jnp.float32)
    ig = ig.astype(jnp.float32) + b_if[:M_HEADS]
    fg = fg.astype(jnp.float32) + b_if[M_HEADS:]
    ig = GATE_CAP * jnp.tanh(ig / GATE_CAP)
    fg = GATE_CAP * jnp.tanh(fg / GATE_CAP)
    ii = ig.reshape(bsz, nc, M_CHUNK, M_HEADS).transpose(0, 3, 1, 2)
    logf = jax.nn.log_sigmoid(fg).reshape(bsz, nc, M_CHUNK, M_HEADS).transpose(0, 3, 1, 2)

    bcum = jnp.cumsum(logf, axis=-1)
    b_last = bcum[..., -1]

    a = b_last[..., None] - bcum + ii
    m_loc = jnp.max(a, axis=-1)
    wgt = jnp.exp(a - m_loc[..., None])
    c_loc = jnp.einsum('bhcl,bhcld,bhcle->bhcde', wgt, k, v)
    n_loc = jnp.einsum('bhcl,bhcld->bhcd', wgt, k)

    def step(carry, inp):
        c_st, n_st, m_st = carry
        cl, nl, ml, bl = inp
        m_new = jnp.maximum(bl + m_st, ml)
        s_old = jnp.exp(bl + m_st - m_new)
        s_new = jnp.exp(ml - m_new)
        c_new = s_old[..., None, None] * c_st + s_new[..., None, None] * cl
        n_new = s_old[..., None] * n_st + s_new[..., None] * nl
        return (c_new, n_new, m_new), (c_st, n_st, m_st)

    init = (jnp.zeros((bsz, M_HEADS, M_DK, M_DV), jnp.float32),
            jnp.zeros((bsz, M_HEADS, M_DK), jnp.float32),
            jnp.zeros((bsz, M_HEADS), jnp.float32))
    xs = (jnp.moveaxis(c_loc, 2, 0), jnp.moveaxis(n_loc, 2, 0),
          jnp.moveaxis(m_loc, 2, 0), jnp.moveaxis(b_last, 2, 0))
    _, (c_prev, n_prev, m_prev) = lax.scan(step, init, xs)
    c_prev = jnp.moveaxis(c_prev, 0, 2)
    n_prev = jnp.moveaxis(n_prev, 0, 2)
    m_prev = jnp.moveaxis(m_prev, 0, 2)

    causal = jnp.tril(jnp.ones((M_CHUNK, M_CHUNK), dtype=bool))
    dmat = bcum[..., :, None] - bcum[..., None, :] + ii[..., None, :]
    dmat = jnp.where(causal, dmat, -jnp.inf)
    g_inter = bcum + m_prev[..., None]
    m_j = jnp.maximum(g_inter, jnp.max(dmat, axis=-1))
    decay = jnp.exp(dmat - m_j[..., None])
    scores = jnp.einsum('bhcid,bhcjd->bhcij', q, k) * decay
    inter = jnp.exp(g_inter - m_j)
    num = (inter[..., None] * jnp.einsum('bhcid,bhcde->bhcie', q, c_prev)
           + jnp.einsum('bhcij,bhcje->bhcie', scores, v))
    den = inter * jnp.einsum('bhcid,bhcd->bhci', q, n_prev) + jnp.sum(scores, axis=-1)
    hh = num / jnp.maximum(jnp.abs(den), jnp.exp(-m_j))[..., None]

    hh = hh * lax.rsqrt(jnp.mean(hh * hh, axis=-1, keepdims=True) + EPS)
    hh = hh.transpose(0, 2, 3, 1, 4).reshape(bsz, s, M_HEADS * M_DV)
    hh = hh * hnorm_g.astype(jnp.float32)
    out = jax.nn.sigmoid(o.astype(jnp.float32)) * hh
    return out.astype(h.dtype) @ w_out

def sgu_mixer(h, w_in, b_in, ln_g, ln_b, ws, bs, w_out):
    bsz, s, _ = h.shape
    nc = s // G_CHUNK
    z = jax.nn.gelu(h @ w_in + b_in, approximate=False)
    u, v = jnp.split(z, 2, axis=-1)
    v = layernorm(v, ln_g, ln_b)
    vr = v.reshape(bsz, nc, G_CHUNK, G_GROUPS, G_GROUP)
    wm = ws * jnp.tril(jnp.ones((G_CHUNK, G_CHUNK), ws.dtype))
    sv = jnp.einsum('gts,bnsgc->bntgc', wm, vr) + bs.T[:, :, None]
    y = u * sv.reshape(bsz, s, G_HALF)
    return y @ w_out

def first_inputs(seed: int = 0) -> dict:
    key = jax.random.key(seed)
    ks = jax.random.split(key, 20)
    f32 = jnp.float32
    nrm = lambda k, shape, scale: jax.random.normal(k, shape, f32) * scale
    return {
        "x": nrm(ks[0], (BATCH, SEQ, D_MODEL), 1.0),
        "c": nrm(ks[1], (BATCH, D_MODEL), 1.0),
        "norm_g": 1.0 + nrm(ks[2], (DEPTH, 4, D_MODEL), 0.1),
        "ada_w": nrm(ks[3], (DEPTH, D_MODEL, 6 * D_MODEL), 0.5 * D_MODEL ** -0.5),
        "ada_b": nrm(ks[4], (DEPTH, 6 * D_MODEL), 0.02),
        "ffn_w1": nrm(ks[5], (DEPTH, D_MODEL, FFN_HIDDEN), D_MODEL ** -0.5),
        "ffn_w2": nrm(ks[6], (DEPTH, FFN_HIDDEN, D_MODEL), FFN_HIDDEN ** -0.5),
        "a_w_in": nrm(ks[7], (N_A, D_MODEL, A_IN), D_MODEL ** -0.5),
        "a_b_if": jnp.concatenate([nrm(ks[8], (N_A, M_HEADS), 0.1),
                                   3.0 + nrm(ks[9], (N_A, M_HEADS), 0.5)], axis=-1),
        "a_hnorm_g": 1.0 + nrm(ks[10], (N_A, M_HEADS * M_DV), 0.1),
        "a_w_out": nrm(ks[11], (N_A, M_HEADS * M_DV, D_MODEL), (M_HEADS * M_DV) ** -0.5),
        "b_w_in": nrm(ks[12], (N_B, D_MODEL, G_FFN), D_MODEL ** -0.5),
        "b_b_in": nrm(ks[13], (N_B, G_FFN), 0.02),
        "b_ln_g": 1.0 + nrm(ks[14], (N_B, G_HALF), 0.1),
        "b_ln_b": nrm(ks[15], (N_B, G_HALF), 0.02),
        "b_ws": nrm(ks[16], (N_B, G_GROUPS, G_CHUNK, G_CHUNK), G_CHUNK ** -0.5),
        "b_bs": 1.0 + nrm(ks[17], (N_B, G_GROUPS, G_CHUNK), 0.1),
        "b_w_out": nrm(ks[18], (N_B, G_HALF, D_MODEL), G_HALF ** -0.5),
    }

def first_block(x, c, norm_g, ada_w, ada_b, ffn_w1, ffn_w2,
              a_w_in, a_b_if, a_hnorm_g, a_w_out,
              b_w_in, b_b_in, b_ln_g, b_ln_b, b_ws, b_bs, b_w_out):
    c_act = jax.nn.silu(c)
    for i in range(DEPTH):
        mod = c_act @ ada_w[i] + ada_b[i]
        sh1, sc1, g1, sh2, sc2, g2 = jnp.split(mod[:, None, :], 6, axis=-1)
        h = rmsnorm(x, norm_g[i, 0]) * (1.0 + sc1) + sh1
        j = i // N_MIXERS
        if i % N_MIXERS == 0:
            y = mlstm_mixer(h, a_w_in[j], a_b_if[j], a_hnorm_g[j], a_w_out[j])
        else:
            y = sgu_mixer(h, b_w_in[j], b_b_in[j], b_ln_g[j], b_ln_b[j], b_ws[j], b_bs[j], b_w_out[j])
        x = x + g1 * rmsnorm(y, norm_g[i, 1])
        h = rmsnorm(x, norm_g[i, 2]) * (1.0 + sc2) + sh2
        y = jnp.square(jax.nn.relu(h @ ffn_w1[i])) @ ffn_w2[i]
        x = x + g2 * rmsnorm(y, norm_g[i, 3])
    return x


DEPTH_2 = 1

CHUNK = 64
Q_BLOCK = 128
ATT_HEADS = 8
ATT_HEAD_DIM = 64
ATT_WIDTH = ATT_HEADS * ATT_HEAD_DIM
IDX_HEADS = 8
IDX_DIM = 64
TOPK_MAX = 256
REL_BUCKETS = 32
REL_MAX_DIST = 1024
CONV_CH = 512
CONV_WIDTH = 31
N_BRANCH = 2
PEER_HEADS = 8
N_KEYS = 128
N_EXPERTS = N_KEYS * N_KEYS
PEER_QDIM = 256
PEER_HALF = PEER_QDIM // 2
PEER_TOPK = 16
PEER_TOKEN_BLOCK = 128
PLE_DIM = 256

IN_WIDTHS = (ATT_WIDTH, ATT_WIDTH, ATT_WIDTH, IDX_HEADS * IDX_DIM, IDX_DIM, IDX_HEADS, 2 * CONV_CH, N_BRANCH * D_MODEL)
IN_TOTAL = 3 * ATT_WIDTH + IDX_HEADS * IDX_DIM + IDX_DIM + IDX_HEADS + 2 * CONV_CH + N_BRANCH * D_MODEL


def _split_points():
    pts, acc = [], 0
    for w in IN_WIDTHS[:-1]:
        acc += w
        pts.append(acc)
    return pts

def rms_norm(x, g):
    x32 = x.astype(jnp.float32)
    y = x32 * lax.rsqrt(jnp.mean(x32 * x32, axis=-1, keepdims=True) + EPS)
    return (y * g.astype(jnp.float32)).astype(x.dtype)

def layer_norm(x, g, b):
    x32 = x.astype(jnp.float32)
    mu = jnp.mean(x32, axis=-1, keepdims=True)
    xc = x32 - mu
    y = xc * lax.rsqrt(jnp.mean(xc * xc, axis=-1, keepdims=True) + EPS)
    return (y * g.astype(jnp.float32) + b.astype(jnp.float32)).astype(x.dtype)

def t5_bucket(rel):
    half = REL_BUCKETS // 2
    max_exact = half // 2
    ret = jnp.where(rel > 0, half, 0)
    n = jnp.abs(rel)
    nf = jnp.maximum(n, 1).astype(jnp.float32)
    large = max_exact + (jnp.log(nf / max_exact) / math.log(REL_MAX_DIST / max_exact) * (half - max_exact)).astype(jnp.int32)
    large = jnp.minimum(large, half - 1)
    return ret + jnp.where(n < max_exact, n, large)

def dsa_attention(q, k, v, qi, ki, wi, rel_bias):
    B, S = q.shape[0], q.shape[1]
    topk = min(TOPK_MAX, S // 4)
    nb = S // Q_BLOCK
    key_chunk = jnp.arange(S, dtype=jnp.int32) // CHUNK
    scale = ATT_HEAD_DIM ** -0.5
    idx_scale = (IDX_DIM ** -0.5) * (IDX_HEADS ** -0.5)

    def blockify(a):
        return jnp.moveaxis(a.reshape((B, nb, Q_BLOCK) + a.shape[2:]), 1, 0)

    def one_block(args):
        qb, qib, wib, qpos = args
        qchunk = qpos // CHUNK
        dots = jax.nn.relu(jnp.einsum('bqhd,bsd->bqhs', qib, ki))
        score = jnp.einsum('bqhs,bqh->bqs', dots, wib) * idx_scale
        visible = key_chunk[None, :] <= qchunk[:, None]
        score = jnp.where(visible[None], score, -jnp.inf)
        _, sel = lax.top_k(score, topk)
        kg = jax.vmap(lambda kk, ii: kk[ii])(k, sel)
        vg = jax.vmap(lambda vv, ii: vv[ii])(v, sel)
        logits = jnp.einsum('bqhd,bqkhd->bqhk', qb, kg).astype(jnp.float32) * scale
        bias = rel_bias[t5_bucket(sel - qpos[None, :, None])]
        logits = logits + jnp.transpose(bias, (0, 1, 3, 2)).astype(jnp.float32)
        ok = (sel // CHUNK) <= qchunk[None, :, None]
        logits = jnp.where(ok[:, :, None, :], logits, -jnp.inf)
        probs = jax.nn.softmax(logits, axis=-1).astype(vg.dtype)
        return jnp.einsum('bqhk,bqkhd->bqhd', probs, vg)

    qpos_blocks = jnp.arange(S, dtype=jnp.int32).reshape(nb, Q_BLOCK)
    out = lax.map(one_block, (blockify(q), blockify(qi), blockify(wi), qpos_blocks))
    return jnp.moveaxis(out, 0, 1).reshape(B, S, ATT_WIDTH)

def conformer_conv(glu_in, conv_w, conv_b, ln_g, ln_b, w_proj):
    a, g = jnp.split(glu_in, 2, axis=-1)
    u = a * jax.nn.sigmoid(g)
    y = lax.conv_general_dilated(u, conv_w, window_strides=(1,), padding=[(CONV_WIDTH - 1, 0)],
                                 dimension_numbers=('NWC', 'WIO', 'NWC'), feature_group_count=CONV_CH)
    y = layer_norm(y + conv_b, ln_g, ln_b)
    return jax.nn.silu(y) @ w_proj

def peer(h, w_query, sub_keys, expert_u, expert_v):
    B, S, D = h.shape
    q = (h @ w_query).reshape(B, S, PEER_HEADS, 2, PEER_HALF)
    sc = jnp.einsum('bshcd,hckd->bshck', q, sub_keys)
    sv, si = lax.top_k(sc, PEER_TOPK)
    n_cand = PEER_TOPK * PEER_TOPK
    cand_s = (sv[..., 0, :, None] + sv[..., 1, None, :]).reshape(B, S, PEER_HEADS, n_cand)
    cand_i = (si[..., 0, :, None] * N_KEYS + si[..., 1, None, :]).reshape(B, S, PEER_HEADS, n_cand)
    top_s, top_j = lax.top_k(cand_s, PEER_TOPK)
    eidx = jnp.take_along_axis(cand_i, top_j, axis=-1)
    gate = jax.nn.softmax(top_s.astype(jnp.float32), axis=-1).astype(h.dtype)
    n_sel = PEER_HEADS * PEER_TOPK
    nb = (B * S) // PEER_TOKEN_BLOCK
    hb = h.reshape(nb, PEER_TOKEN_BLOCK, D)
    eb = eidx.reshape(nb, PEER_TOKEN_BLOCK, n_sel)
    gb = gate.reshape(nb, PEER_TOKEN_BLOCK, n_sel)

    def one_block(args):
        xt, et, gt = args
        u = expert_u[et]
        v = expert_v[et]
        act = jax.nn.gelu(jnp.einsum('tnd,td->tn', u, xt)) * gt
        return jnp.einsum('tn,tnd->td', act, v)

    return lax.map(one_block, (hb, eb, gb)).reshape(B, S, D)

def second_inputs(seed: int = 0) -> dict:
    key = jax.random.key(seed)
    ks = jax.random.split(key, 24)
    f = jnp.float32

    def nrm(k, shape, scale):
        return jax.random.normal(k, shape, f) * scale

    def gain(k, shape):
        return 1.0 + 0.05 * jax.random.normal(k, shape, f)

    return {
        'x': nrm(ks[0], (BATCH, SEQ, D_MODEL), 1.0),
        'p': nrm(ks[1], (DEPTH_2, BATCH, SEQ, PLE_DIM), 1.0),
        'rel_bias': nrm(ks[2], (REL_BUCKETS, ATT_HEADS), 0.1),
        'attn_norm_g': gain(ks[3], (DEPTH_2, D_MODEL)),
        'w_in': nrm(ks[4], (DEPTH_2, D_MODEL, IN_TOTAL), D_MODEL ** -0.5),
        'b_gate': nrm(ks[5], (DEPTH_2, N_BRANCH * D_MODEL), 0.02),
        'q_norm_g': gain(ks[6], (DEPTH_2, ATT_HEAD_DIM)),
        'k_norm_g': gain(ks[7], (DEPTH_2, ATT_HEAD_DIM)),
        'w_att_out': nrm(ks[8], (DEPTH_2, ATT_WIDTH, D_MODEL), ATT_WIDTH ** -0.5),
        'conv_w': nrm(ks[9], (DEPTH_2, CONV_WIDTH, 1, CONV_CH), CONV_WIDTH ** -0.5),
        'conv_b': nrm(ks[10], (DEPTH_2, CONV_CH), 0.02),
        'conv_ln_g': gain(ks[11], (DEPTH_2, CONV_CH)),
        'conv_ln_b': nrm(ks[12], (DEPTH_2, CONV_CH), 0.02),
        'w_conv_out': nrm(ks[13], (DEPTH_2, CONV_CH, D_MODEL), CONV_CH ** -0.5),
        'w_out': nrm(ks[14], (DEPTH_2, D_MODEL, D_MODEL), D_MODEL ** -0.5),
        'ffn_norm_g': gain(ks[15], (DEPTH_2, D_MODEL)),
        'w_peer_q': nrm(ks[16], (DEPTH_2, D_MODEL, PEER_HEADS * PEER_QDIM), D_MODEL ** -0.5),
        'peer_sub_keys': nrm(ks[17], (DEPTH_2, PEER_HEADS, 2, N_KEYS, PEER_HALF), PEER_HALF ** -0.5),
        'peer_u': nrm(ks[18], (DEPTH_2, N_EXPERTS, D_MODEL), D_MODEL ** -0.5),
        'peer_v': nrm(ks[19], (DEPTH_2, N_EXPERTS, D_MODEL), PEER_HEADS ** -0.5),
        'ple_norm_g': gain(ks[20], (DEPTH_2, D_MODEL)),
        'w_ple_gate': nrm(ks[21], (DEPTH_2, D_MODEL, D_MODEL), D_MODEL ** -0.5),
        'w_ple_proj': nrm(ks[22], (DEPTH_2, PLE_DIM, D_MODEL), PLE_DIM ** -0.5),
    }

def second_block(x, p, rel_bias, attn_norm_g, w_in, b_gate, q_norm_g, k_norm_g, w_att_out,
              conv_w, conv_b, conv_ln_g, conv_ln_b, w_conv_out, w_out, ffn_norm_g,
              w_peer_q, peer_sub_keys, peer_u, peer_v, ple_norm_g, w_ple_gate, w_ple_proj):
    B, S, D = x.shape
    for i in range(DEPTH_2):
        h = rms_norm(x, attn_norm_g[i])
        proj = h @ w_in[i]
        q, k, v, qi, ki, wi, glu_in, gates = jnp.split(proj, _split_points(), axis=-1)
        q = rms_norm(q.reshape(B, S, ATT_HEADS, ATT_HEAD_DIM), q_norm_g[i])
        k = rms_norm(k.reshape(B, S, ATT_HEADS, ATT_HEAD_DIM), k_norm_g[i])
        v = v.reshape(B, S, ATT_HEADS, ATT_HEAD_DIM)
        qi = qi.reshape(B, S, IDX_HEADS, IDX_DIM)
        y_att = dsa_attention(q, k, v, qi, ki, wi, rel_bias) @ w_att_out[i]
        y_conv = conformer_conv(glu_in, conv_w[i], conv_b[i], conv_ln_g[i], conv_ln_b[i], w_conv_out[i])
        g = jax.nn.sigmoid(gates + b_gate[i]).reshape(B, S, N_BRANCH, D)
        mixed = g[:, :, 0, :] * y_att + g[:, :, 1, :] * y_conv
        x = x + mixed @ w_out[i]
        h2 = rms_norm(x, ffn_norm_g[i])
        x = x + peer(h2, w_peer_q[i], peer_sub_keys[i], peer_u[i], peer_v[i])
        h3 = rms_norm(x, ple_norm_g[i])
        x = x + jax.nn.sigmoid(h3 @ w_ple_gate[i]) * (p[i] @ w_ple_proj[i])
    return x


def setup_inputs(seed=0):
    out = dict(first_inputs(seed))
    for name, value in second_inputs(seed + 1).items():
        if name != "x":
            out[name + "_2"] = value
    return out


def reference(
    x, c, norm_g, ada_w, ada_b, ffn_w1, ffn_w2, a_w_in, a_b_if, a_hnorm_g, a_w_out, b_w_in,
    b_b_in, b_ln_g, b_ln_b, b_ws, b_bs, b_w_out, p_2, rel_bias_2, attn_norm_g_2, w_in_2,
    b_gate_2, q_norm_g_2, k_norm_g_2, w_att_out_2, conv_w_2, conv_b_2, conv_ln_g_2, conv_ln_b_2,
    w_conv_out_2, w_out_2, ffn_norm_g_2, w_peer_q_2, peer_sub_keys_2, peer_u_2, peer_v_2,
    ple_norm_g_2, w_ple_gate_2, w_ple_proj_2,
):
    x = first_block(
        x, c, norm_g, ada_w, ada_b, ffn_w1, ffn_w2, a_w_in, a_b_if, a_hnorm_g, a_w_out, b_w_in,
        b_b_in, b_ln_g, b_ln_b, b_ws, b_bs, b_w_out,
    )
    return second_block(
        x, p_2, rel_bias_2, attn_norm_g_2, w_in_2, b_gate_2, q_norm_g_2, k_norm_g_2,
        w_att_out_2, conv_w_2, conv_b_2, conv_ln_g_2, conv_ln_b_2, w_conv_out_2, w_out_2,
        ffn_norm_g_2, w_peer_q_2, peer_sub_keys_2, peer_u_2, peer_v_2, ple_norm_g_2,
        w_ple_gate_2, w_ple_proj_2,
    )


_drawn_inputs = setup_inputs


def setup_inputs(seed=0):
    import zlib

    import numpy as np

    out = dict(_drawn_inputs(seed))
    spreads = {}
    factors = {'b_b_in': 3.69,
     'b_ln_b': 4.771,
     'rel_bias_2': 3.916,
     'b_gate_2': 7.805,
     'q_norm_g_2': 6.201,
     'k_norm_g_2': 6.072,
     'conv_b_2': 3.092,
     'conv_ln_b_2': 4.4,
     'ple_norm_g_2': 7.224}
    for name, (base, spread) in spreads.items():
        noise = np.random.default_rng([zlib.crc32(name.encode()), seed]).standard_normal(out[name].shape)
        drawn = base * np.exp(spread * noise) if base else spread * noise
        out[name] = __import__('jax').numpy.asarray(drawn.astype(out[name].dtype))
    for name, factor in factors.items():
        out[name] = (out[name] * factor).astype(out[name].dtype)
    return out
```

```python
from contextlib import ExitStack

import concourse.bass as bass
from concourse import mybir

ALU = mybir.AluOpType
ACT = mybir.ActivationFunctionType
F32 = mybir.dt.float32
U32 = mybir.dt.uint32
AX_X = mybir.AxisListType.X

P = 128
TOK = 256
TT = TOK // P
D = 1024
DC = D // P
H = 8
DK, DV = 64, 128
FF = 4096
GH = 2048
GG = GH // P
AH = 64
CH = 512
TAPS = 31
TOPK = 64
HC = 2 * H
PK = 16
NSEL = H * PK
NKEYS = 128
RELS = 384
EPS = 1e-6
CAP = 15.0
NEG = -1e30
TAKEN = -3e38

RING = 4
UNIT = 4096
GBUF = 8

UNITS = [("ada0a", 4), ("a_qk", 2), ("a_v", 2), ("a_o", 2), ("ada0b", 2), ("ada0c", 2), ("ada0d", 2),
         ("ada0e", 2), ("a_out", 2), ("ada1a", 4), ("up0", 8), ("down0", 8), ("ada1b", 4), ("b_u", 4),
         ("b_v", 4), ("ada1c", 4), ("b_out", 4), ("up1", 8), ("down1", 8), ("qi", 1), ("qkv", 3),
         ("glu", 2), ("gates", 4), ("att", 1), ("conv", 1), ("out", 2), ("peer_q", 4), ("ple", 2)]
FEWER = {"down0": 2, "down1": 2, "b_out": 2, "att": 2, "conv": 2, "ple": 4}
BLOCKS = [(name, FEWER.get(name, n)) for name, n in UNITS]
ADA = {"ada0a": (0, 0), "ada0b": (0, 4), "ada0c": (0, 6), "ada0d": (0, 8), "ada0e": (0, 10),
       "ada1a": (1, 0), "ada1b": (1, 4), "ada1c": (1, 8)}
TURNS = [("norm0", 4), ("k_tok", 1), ("n_loc", 1), ("scoreT", 4), ("qn", 1), ("mix_a", 4),
         ("norm1", 4), ("norm2", 4), ("norm3", 4), ("norm4", 4), ("qT", 2), ("kT", 2), ("probT", 6),
         ("conv_tok", 2), ("convT", 2), ("mix_c", 4), ("norm5", 4), ("norm6", 4)]
SPARES = [("rel", 1), ("gates", 1), ("cum", 1), ("rb", 2), ("score", 2), ("c_loc", 1), ("pv0", 1),
          ("qc", 1), ("pv1", 1), ("sv", 4), ("kiwi", 1), ("dots", 3), ("logit", 3), ("att", 1),
          ("psc", 4)]


def starts(table):
    out, at = {}, 0
    for name, n in table:
        out[name] = at
        at += n
    out["end"] = at
    return out


UNIT0, BLOCK0, TURN0, SPARE0 = starts(UNITS), starts(BLOCKS), starts(TURNS), starts(SPARES)


def signal(name, i):
    if name in ("down0", "down1"):
        return "unit_used", UNIT0[name] + 4 * i + 4
    if name == "b_out":
        return "unit_used", UNIT0[name] + 2 * i + 2
    if name in ("att", "conv"):
        return ("half_done", 1 + (name == "conv")) if i == 0 else ("unit_used", UNIT0[name] + 1)
    if name == "peer_q":
        return ("tile0_queries", i + 1) if i < 2 else ("unit_used", UNIT0[name] + 2 * i - 2)
    if name == "ple":
        return ("proj_done", "ple_gate")[i % 2], i // 2 + 1
    return "unit_used", UNIT0[name] + i + 1


def bcast(ap, axis, n):
    v = ap.unsqueeze(axis)
    shape = list(v.shape)
    shape[axis] = n
    return v.to_broadcast(shape)


def build(nc, A, out):
    with ExitStack() as ctx:
        sems = {}

        def sem(name):
            if name not in sems:
                sems[name] = ctx.enter_context(nc.semaphore(name))
            return sems[name]

        def sb(name, shape, dt=F32):
            return ctx.enter_context(nc.sbuf_tensor(name, shape, dt))

        ring = sb("ring", [P, RING, UNIT])
        mod = sb("mod", [P, 2, 6 * D])
        xs = sb("xs", [P, TT, D])
        hT = sb("hT", [P, DC, TOK])
        ybuf = sb("ybuf", [P, TT, D])
        rows2 = sb("rows2", [P, 2, D])
        arena = sb("arena", [P, 12808])
        consts = sb("consts", [P, 7 * P + 16])
        ones = sb("ones", [P, P])
        wgate = sb("wgate", [P, DC, 16])
        bif = sb("bif", [P, 16])
        ncols = sb("ncols", [P, 7, DC])
        small = sb("small", [P, 1216])
        cB = sb("cB", [P, DC, P])

        ident = consts[:, 0:P]
        upper = consts[:, P:2 * P]
        causal = consts[:, 2 * P:3 * P]
        flip = consts[:, 3 * P:4 * P]
        visible = [consts[:, 4 * P:5 * P], consts[:, 5 * P:7 * P]]
        iota16 = consts[:, 7 * P:]

        def carve(buf, start, dims):
            n = 1
            for d in dims:
                n *= d
            v = buf[:, start:start + n]
            if len(dims) == 2:
                v = v.rearrange("p (a b) -> p a b", a=dims[0])
            elif len(dims) == 3:
                v = v.rearrange("p (a b c) -> p a b c", a=dims[0], b=dims[1])
            elif len(dims) == 4:
                v = v.rearrange("p (a b c d) -> p a b c d", a=dims[0], b=dims[1], c=dims[2])
            return v

        at = [0]

        def tiny(*dims):
            n = 1
            for d in dims:
                n *= d
            v = carve(small, at[0], dims)
            at[0] += n
            assert at[0] <= 1216, at[0]
            return v

        epsc = tiny(1)
        onec = tiny(1)
        ss, std, rstd = tiny(TT), tiny(TT), tiny(TT)
        mcol = tiny(2, 4, DC)
        scol = tiny(4, DC)
        ccol, csig, cact = tiny(DC), tiny(DC), tiny(DC)
        gth = tiny(TT, 16)
        gin = tiny(TT, 16)
        gii, gex, glf = tiny(TT, H), tiny(TT, H), tiny(TT, H)
        gcum = tiny(TT, 2, H)
        gr = tiny(TT, H)
        maxr, rowm, mprev, mx, nmx = tiny(TT, H), tiny(TT, H), tiny(TT, H), tiny(TT, H), tiny(TT, H)
        dif, einter, enm, mj = tiny(TT, H), tiny(TT, H), tiny(TT, H), tiny(TT, H)
        wdif, wgt = tiny(H), tiny(H)
        rsum, den, dabs, dinv = tiny(TT, H), tiny(TT, H), tiny(TT, H), tiny(TT, H)
        qnv, ssn, ssd, hroot, hfac = tiny(H), tiny(TT, H), tiny(TT, H), tiny(TT, H), tiny(TT, H)
        bst = tiny(4, 6)
        mv = tiny(TT, 2)
        lnstd, lnr = tiny(TT), tiny(TT)
        bucol = tiny(GG)
        qss, qroot, qrec = tiny(2, TT, H), tiny(2, TT, H), tiny(2, TT, H)
        qgain, kgain = tiny(AH), tiny(AH)
        wi = tiny(TT, H)
        top8 = tiny(8)
        lmax, lneg, lsum, lrec = tiny(TT, H), tiny(TT, H), tiny(TT, H), tiny(TT, H)
        cwcol, cbcol = tiny(CH // P, TAPS), tiny(CH // P)

        qT = carve(arena, 0, (4, TOK))
        kT = carve(arena, 1024, (4, TOK))
        vtok = carve(arena, 2048, (TT, H, DV))
        osig = carve(arena, 4096, (TT, D))
        dec = carve(arena, 6144, (TT, H, P))
        decT = carve(arena, 8192, (TT, H, P))
        diag = carve(arena, 8192, (TT, H, P))
        kw = carve(arena, 10240, (4 * P,))
        cbd = carve(arena, 10752, (4, 2 * DV))
        nbd = carve(arena, 11776, (4, 2))
        qc = carve(arena, 11784, (H, DV))
        hnrow = carve(arena, 10752, (D,))
        relwork = carve(arena, 11784, (RELS,))
        onehot = carve(arena, 12168, (RELS,))[0:32, :]
        relb = carve(arena, 12552, (H,))[0:32, :]
        fT = carve(arena, 0, (FF // P, TOK))
        frelu = carve(arena, 8192, (2, 4, TOK))
        uT = carve(arena, 0, (GG, TOK))
        vsg = carve(arena, 4096, (TT, GH))
        wsT = carve(arena, 8192, (GG, P))
        svb = carve(arena, 10240, (H, P))
        modf = mod[:, :, :].rearrange("p l n -> p (l n)")
        lng, lnb, bsrow = carve(modf, 0, (GH,)), carve(modf, 2048, (GH,)), carve(modf, 4096, (GG, P))
        bvrow = ybuf[:, :, :].rearrange("p a b -> p (a b)")
        gates = carve(modf, 0, (TT, 2 * D))
        bgrow = carve(modf, 4096, (2 * D,))
        relH = carve(modf, 6144, (H, TOK))
        logit = carve(modf, 8192, (H, TOK))
        wkiwi = carve(modf, 10240, (DC, 2 * AH + H))
        qtok = carve(arena, 0, (TT, 512))
        ktok = carve(arena, 1024, (TT, 512))
        vatt = carve(arena, 2048, (TT, 512))
        qiT = carve(arena, 3072, (4, TOK))
        kiT = carve(arena, 4096, (TOK,))
        q2T = carve(arena, 4352, (4, TOK))
        k2T = carve(arena, 5376, (4, TOK))
        rel8 = carve(arena, 6400, (4, TOK))
        score = carve(arena, 7424, (TT, TOK))
        prT = carve(arena, 7936, (3, H, P))
        aT = carve(arena, 7936, (4, TOK))
        qsq = carve(arena, 8960, (TT, 512))
        attT = carve(arena, 4352, (4, TOK))
        upad = carve(arena, 11008, (CH // P, TOK + TAPS - 1))
        ycT = carve(arena, 0, (4, TOK))
        yct = carve(arena, 1024, (TT, CH))
        ysg = carve(arena, 3072, (TT, CH))
        clng = carve(arena, 12152, (CH,))
        clnb = carve(arena, 6400, (CH,))
        cT = carve(arena, 5376, (4, TOK))
        pqT = carve(arena, 0, (HC, TOK))
        skT = carve(arena, 4096, (HC, NKEYS))
        psc = carve(arena, 6144, (HC, NKEYS))
        cand = carve(arena, 8192, (H, PK, PK))
        h2 = carve(arena, 10240, (TT, D))
        gbufs = [carve(modf, 0, (4, D)), carve(arena, 0, (4, D))]
        eqc = carve(modf, 4096, (H, PK, PK))
        ptT = carve(modf, 8192, (2, TOK))
        sig = carve(modf, 9600, (TT, D))
        wproj = carve(modf, 4096, (2, D))
        fgrow = rows2[:, 0, :]
        sv = carve(modf, 6144, (H, 2, PK))
        sif = carve(modf, 6400, (H, 2, PK))
        topv = carve(modf, 6656, (H, PK))
        tjf = carve(modf, 6784, (2, H, PK))
        i12 = carve(modf, 7040, (2, H, PK))
        gateT = carve(modf, 7296, (TT, NSEL))
        dots = carve(modf, 7552, (TT, NSEL))
        actv = carve(modf, 7808, (TT, NSEL))
        siu = carve(modf, 8704, (H, 2, PK)).bitcast(U32)
        tju = carve(modf, 8960, (3, H, PK)).bitcast(U32)
        eidx = carve(modf, 9344, (TT, NSEL)).bitcast(U32)
        gmax, gsum, grec = tiny(H), tiny(H), tiny(H)
        icur = sb("icur", [P, GBUF], U32)

        rel_dram = nc.dram_tensor("rel_rows", (H, RELS), F32, kind="Internal").ap()

        G = ctx.enter_context(nc.psum_tensor("G", [P, 2, 2, 512], F32))
        T = ctx.enter_context(nc.psum_tensor("T", [P, 2, 512], F32))
        M = ctx.enter_context(nc.psum_tensor("M", [P, 2, 512], F32))
        M8 = M[:, :, :].rearrange("p b (j n) -> p (b j) n", n=P)
        MP = M[:, :, :].rearrange("p b (j n) -> p b j n", n=P)

        ring_full = [sem(f"ring_full{i}") for i in range(RING)]
        unit_used = sem("unit_used")
        g_free = [sem("g_free0"), sem("g_free1")]
        t_ready = sem("t_ready")
        t_free = [sem("t_free0"), sem("t_free1")]
        m_ready, m_free = sem("m_ready"), sem("m_free")

        block = ctx.enter_context(nc.Block())

        def block_done(eng, name, i):
            what, count = signal(name, i)
            eng.wait_ge(sem(what), count)
            return BLOCK0[name] + i

        def read_out(eng, name, i):
            b = BLOCK0[name] + i
            eng.wait_ge(g_free[b % 2], b // 2 + 1)

        def Gc(b):
            return G[:, b, :, :].rearrange("p a (c n) -> p (a c) n", n=TOK)

        def par(vals):
            return vals.rearrange("p (j b) n -> p b j n", b=2)

        @block.sync
        def _(sp):
            sp.dma_start(ccol, A["c"]).then_inc(sem("l_c"), 16)
            for u in range(RING):
                sp.dma_start(ring[:, u, :], A["wpack"][u]).then_inc(ring_full[u], 16)
                if u == 1:
                    sp.dma_start(xs[:, :, :], A["x"].rearrange("(t p) d -> p t d", p=P)).then_inc(sem("x_loaded"), 16)
            with sp.Fori(1, UNIT0["end"] // RING) as i:
                for j in range(RING):
                    sp.wait_ge(unit_used, RING * i + (j - RING + 1))
                    sp.dma_start(ring[:, j, :], A["wpack"][RING * i + j]).then_inc(ring_full[j], 16)
            for t in range(TT):
                sp.wait_ge(sem("out_done"), t + 1)
                sp.dma_start(out[t * P:(t + 1) * P, :], xs[:, t, :]).then_inc(sem("stored"), 16)
            sp.wait_ge(sem("stored"), 32)

        @block.gpsimd
        def _(pool):
            def load(dst, src, name):
                pool.dma_start(dst, src).then_inc(sem(name), 16)

            load(consts[:, :], A["consts"], "l_consts")
            load(onehot[:, :], A["onehot"], "l_rel")
            load(relb[:, :], A["rel_bias"], "l_rel")
            load(mod[:, 0, :], A["ada_b"][0].partition_broadcast(P), "l_mod0")
            load(ncols[:, :, :], A["ncols"], "l_ncols")
            load(wgate[:, :, :], A["wgate"], "l_wgate")
            load(bif[:, :], A["b_if"].partition_broadcast(P), "l_bif")
            load(rows2[:, 0, :], A["norm_g"][0, 1].partition_broadcast(P), "l_rows2")
            load(rows2[:, 1, :], A["norm_g"][0, 3].partition_broadcast(P), "l_rows2")
            load(hnrow, A["hnorm_g"].partition_broadcast(P), "l_hnorm")
            for dst, name in ((qgain, "q_norm_g"), (kgain, "k_norm_g")):
                load(dst, A[name].partition_broadcast(P), "l_small")
            for dst, name in ((cwcol, "conv_w"), (cbcol, "conv_b"), (bucol, "bu")):
                load(dst, A[name], "l_small")
            load(mod[:, 1, :], A["ada_b"][1].partition_broadcast(P), "l_mod1")
            pool.wait_ge(m_free, SPARE0["rel"] + 1)
            pool.dma_start(rel_dram, relwork[0:H, :]).then_inc(sem("rel_out"), 16)
            pool.wait_ge(sem("rel_out"), 16)
            pool.wait_ge(sem("gains"), 2)
            load(rows2[:, 0, :], A["norm_g"][1, 1].partition_broadcast(P), "l_rows2")
            load(rows2[:, 1, :], A["norm_g"][1, 3].partition_broadcast(P), "l_rows2")
            pool.wait_ge(sem("x_ready"), 2)
            load(wsT, A["wsT"], "l_ws")
            load(lng, A["ln_g"].partition_broadcast(P), "l_sgu")
            load(lnb, A["ln_b"].partition_broadcast(P), "l_sgu")
            load(bsrow.rearrange("p a b -> p (a b)"), A["bs"].partition_broadcast(P), "l_sgu")
            for n in (TURN0["norm2"] + 2, TURN0["norm2"] + 3):
                pool.wait_ge(t_free[n % 2], n // 2 + 1)
            load(bvrow, A["bv"].partition_broadcast(P), "l_bv")
            pool.wait_ge(sem("x_ready"), 4)
            load(wkiwi, A["wkiwi"], "l_kiwi")
            load(bgrow, A["b_gate"].partition_broadcast(P), "l_bgate")
            load(relH, bass.AP(rel_dram.tensor, 0, [[1, P], [RELS, H], [1, TOK]]), "l_relh")
            load(fgrow, A["ffn_norm_g"].partition_broadcast(P), "l_fg")
            load(clng, A["conv_ln_g"].partition_broadcast(P), "l_cln")
            pool.wait_ge(sem("glu_done"), 1)
            load(clnb, A["conv_ln_b"].partition_broadcast(P), "l_cln")
            for i in range(2):
                read_out(pool, "out", i)
            load(skT, A["skT"], "l_sk")
            load(ptT, A["pT"], "l_pt")
            for t in range(TT):
                pool.wait_ge(sem("eidx_ready"), t + 1)
                if t == 0:
                    pool.wait_ge(m_ready, SPARE0["psc"] + 4)
                if t == 1:
                    load(wproj, A["w_ple_proj"], "l_proj")
                for kind, table in ((0, A["peer_u"]), (1, A["peer_v"])):
                    base = (2 * t + kind) * NSEL
                    with pool.Fori(0, NSEL // GBUF) as i:
                        for j in range(GBUF):
                            pool.wait_ge(sem("row_used"), GBUF * i + (base + j + 1))
                            nc.gpsimd.tensor_copy(icur[:, j:j + 1], eidx[:, t, bass.ds(GBUF * i + j, 1)]).then_inc(sem("icur"), 1)
                            pool.wait_ge(sem("icur"), GBUF * i + (base + j + 1))
                            pool.nop(nofuse=True)
                            nc.gpsimd.indirect_dma_start(
                                out=gbufs[j // 4][:, j % 4, :], out_offset=None, in_=table,
                                in_offset=bass.IndirectOffsetOnAxis(ap=icur[:, j:j + 1], axis=0),
                            ).then_inc(sem(f"row{j}"), 16)

        @block.scalar
        def _(act):
            n_act = [0]

            def link(ins):
                n_act[0] += 1
                ins.then_inc(sem("act_step"), 1)
                act.wait_ge(sem("act_step"), n_act[0])

            def norm(n):
                if n == 0:
                    act.wait_ge(sem("x_loaded"), 16)
                    act.wait_ge(sem("consts_set"), 2)
                elif n == 5:
                    for i in range(2):
                        read_out(act, "out", i)
                else:
                    act.wait_ge(sem("x_ready"), min(n, 5))
                for t in range(TT):
                    link(nc.scalar.activation(ybuf[:, t, :], xs[:, t, :], ACT.Square, accum_out=ss[:, t:t + 1]))
                nc.scalar.activation(std, ss, ACT.Sqrt, bias=epsc, scale=1.0 / D).then_inc(sem("norm_std"), 1)
                act.wait_ge(sem("norm_rstd"), n + 1)
                for t in range(TT):
                    nc.scalar.activation(ybuf[:, t, :], xs[:, t, :], ACT.Copy,
                                         scale=rstd[:, t:t + 1]).then_inc(sem("norm_xhat"), 1)

            def post(name):
                for nb in range(2):
                    b = block_done(act, name, nb)
                    nc.scalar.activation(ybuf[:, :, nb * 512:(nb + 1) * 512], G[:, b % 2, :, :],
                                         ACT.Copy).then_inc(g_free[b % 2], 1)
                for nb in range(2):
                    read_out(act, name, nb)
                for t in range(TT):
                    link(nc.scalar.activation(hT[:, 4 * t:4 * t + 4, :].rearrange("p a b -> p (a b)"), ybuf[:, t, :],
                                              ACT.Square, accum_out=ss[:, t:t + 1]))
                nc.scalar.activation(std, ss, ACT.Sqrt, bias=epsc, scale=1.0 / D).then_inc(sem("post_std"), 1)

            def ffn(f):
                with act.Fori(0, 2) as i:
                    for j in range(4):
                        act.wait_ge(unit_used, 4 * i + (UNIT0[f"up{f}"] + j + 1))
                        act.wait_ge(sem("relu_free"), 4 * i + (8 * f + j + 1))
                        nc.scalar.activation(frelu[:, j % 2, :, :], Gc(j % 2), ACT.Relu).then_inc(g_free[j % 2], 1)
                post(f"down{f}")

            act.wait_ge(sem("l_c"), 16)
            nc.scalar.activation(csig, ccol, ACT.Sigmoid).then_inc(sem("csig"), 1)
            norm(0)
            act.wait_ge(m_free, SPARE0["gates"] + 1)
            nc.scalar.activation(gth, gin, ACT.Tanh, scale=1.0 / CAP).then_inc(sem("gth"), 1)
            act.wait_ge(sem("gth"), 1)
            link(nc.scalar.activation(gex, gth[:, :, H:], ACT.Exp, scale=-CAP))
            nc.scalar.activation(glf, gex, ACT.Ln, bias=onec).then_inc(sem("glf"), 1)
            for n, (dst, scale) in enumerate(((qT, 1.0), (kT, DK ** -0.5))):
                b = block_done(act, "a_qk", n)
                nc.scalar.activation(dst, Gc(b % 2), ACT.Copy, scale=scale).then_inc(g_free[b % 2], 1)
            act.wait_ge(sem("mx"), 1)
            link(nc.scalar.activation(einter, dif, ACT.Exp))
            link(nc.scalar.activation(enm, mj, ACT.Exp, scale=-1.0))
            nc.scalar.activation(wgt, wdif, ACT.Exp, scale=-1.0).then_inc(sem("wgt"), 1)
            for t in range(TT):
                for h in range(H):
                    nc.scalar.activation(dec[:, t, h, :], dec[:, t, h, :], ACT.Exp,
                                         bias=nmx[:, t, h:h + 1]).then_inc(sem("decay"), 1)
            for nb in range(2):
                b = block_done(act, "a_v", nb)
                nc.scalar.activation(vtok[:, :, 4 * nb:4 * nb + 4, :].rearrange("p t h e -> p t (h e)"),
                                     G[:, b % 2, :, :], ACT.Copy).then_inc(g_free[b % 2], 1)
            for nb in range(2):
                b = block_done(act, "a_o", nb)
                nc.scalar.activation(osig[:, :, nb * 512:(nb + 1) * 512], G[:, b % 2, :, :],
                                     ACT.Sigmoid).then_inc(g_free[b % 2], 1)
            for t in range(TT):
                act.wait_ge(sem("ssd"), t + 1)
                nc.scalar.activation(hroot[:, t, :], ssd[:, t, :], ACT.Sqrt, bias=epsc).then_inc(sem("hroot"), 1)
            post("a_out")
            norm(1)
            ffn(0)
            norm(2)
            act.wait_ge(sem("l_small"), 80)
            for u in range(4):
                b = block_done(act, "b_u", u)
                for c in range(4):
                    ins = nc.scalar.activation(uT[:, 4 * u + c, :], Gc(b % 2)[:, c, :], ACT.Gelu,
                                               bias=bucol[:, 4 * u + c:4 * u + c + 1])
                ins.then_inc(g_free[b % 2], 1)
            for nb in range(4):
                read_out(act, "b_v", nb)
                v = vsg[:, :, nb * 512:(nb + 1) * 512]
                nc.scalar.activation(v, v, ACT.Gelu).then_inc(sem("v_gelu"), 1)
            for t in range(TT):
                act.wait_ge(sem("ln_var"), t + 1)
                nc.scalar.activation(lnstd[:, t:t + 1], mv[:, t, 1:2], ACT.Sqrt, bias=epsc).then_inc(sem("ln_std"), 1)
            post("b_out")
            norm(3)
            ffn(1)
            norm(4)
            b = block_done(act, "qi", 0)
            nc.scalar.activation(qiT, Gc(b % 2), ACT.Copy).then_inc(g_free[b % 2], 1)
            for n, dst in enumerate((qtok, ktok, vatt)):
                b = block_done(act, "qkv", n)
                nc.scalar.activation(dst, G[:, b % 2, :, :], ACT.Copy).then_inc(g_free[b % 2], 1)
            rel0 = rel8.rearrange("p a (b s) -> p (a b) s", s=P)
            act.wait_ge(m_ready, SPARE0["dots"] + 1)
            nc.scalar.activation(rel0.rearrange("p (b j) s -> p b j s", b=2), MP, ACT.Relu).then_inc(m_free, 1)
            for r in range(2):
                act.wait_ge(m_ready, SPARE0["dots"] + r + 2)
                act.wait_ge(sem("dots_done"), r + 1)
                nc.scalar.activation(rel8.rearrange("p (b j) s -> p b j s", b=2),
                                     M[:, :, :].rearrange("p b (j s) -> p b j s", s=TOK),
                                     ACT.Relu).then_inc(m_free, 1)
            b = block_done(act, "glu", 0)
            nc.scalar.activation(aT, Gc(b % 2), ACT.Copy).then_inc(g_free[b % 2], 1)
            b = block_done(act, "glu", 1)
            act.wait_ge(sem("dots_done"), 3)
            nc.scalar.activation(rel8, Gc(b % 2), ACT.Sigmoid).then_inc(g_free[b % 2], 1)
            for a in range(2):
                act.wait_ge(sem("qss"), a + 1)
                nc.scalar.activation(qroot[:, a, :, :], qss[:, a, :, :], ACT.Sqrt, bias=epsc,
                                     scale=1.0 / AH).then_inc(sem("qroot"), 1)
            for nb in range(4):
                read_out(act, "gates", nb)
                v = gates[:, :, nb * 512:(nb + 1) * 512]
                nc.scalar.activation(v, v, ACT.Sigmoid).then_inc(sem("gate_sig"), 1)
            for t in range(TT):
                act.wait_ge(sem("lneg"), t + 1)
                for h in range(H):
                    v = logit[:, h, 0:P * (t + 1)]
                    nc.scalar.activation(v, v, ACT.Exp, bias=lneg[:, t, h:h + 1],
                                         accum_out=lsum[:, t, h:h + 1]).then_inc(sem("probs"), 1)
            for t in range(TT):
                act.wait_ge(sem("cln_var"), t + 1)
                nc.scalar.activation(lnstd[:, t:t + 1], mv[:, t, 1:2], ACT.Sqrt, bias=epsc).then_inc(sem("cln_std"), 1)
            act.wait_ge(sem("cln"), 2)
            nc.scalar.activation(ysg, yct, ACT.Sigmoid).then_inc(sem("ysg"), 1)
            norm(5)

            def queries(t):
                for i in range(2):
                    b = block_done(act, "peer_q", 2 * t + i)
                    nc.scalar.activation(pqT[:, H * i:H * i + H, t * P:(t + 1) * P],
                                         G[:, b % 2, :, :].rearrange("p a (c n) -> p (a c) n", n=P),
                                         ACT.Copy).then_inc(g_free[b % 2], 1)

            def sub_scores(t):
                for r in range(2):
                    act.wait_ge(m_ready, SPARE0["psc"] + 2 * t + r + 1)
                    if t:
                        act.wait_ge(sem("eidx_ready"), t)
                    nc.scalar.activation(psc[:, H * r:H * r + H, :], M8, ACT.Copy).then_inc(m_free, 1)

            def gate_exp(t):
                act.wait_ge(sem("topv"), t + 1)
                nc.scalar.activation(topv, topv, ACT.Exp).then_inc(sem("gate_exp"), 1)

            def expert_gelu(t):
                act.wait_ge(sem("dots_all"), t + 1)
                nc.scalar.activation(actv[:, t, :], dots[:, t, :], ACT.Gelu_apprx_tanh).then_inc(sem("gelu"), 1)

            def embed(t):
                act.wait_ge(sem("x_ready"), 5 + t)
                link(nc.scalar.activation(ybuf[:, t, :], xs[:, t, :], ACT.Square, accum_out=ss[:, t:t + 1]))
                nc.scalar.activation(std[:, t:t + 1], ss[:, t:t + 1], ACT.Sqrt, bias=epsc,
                                     scale=1.0 / D).then_inc(sem("norm_std"), 1)
                act.wait_ge(sem("norm_rstd"), 7 + t)
                nc.scalar.activation(ybuf[:, t, :], xs[:, t, :], ACT.Copy,
                                     scale=rstd[:, t:t + 1]).then_inc(sem("norm_xhat"), 1)
                b = block_done(act, "ple", 2 * t + 1)
                nc.scalar.activation(sig[:, t, :], G[:, b % 2, :, :].rearrange("p a n -> p (a n)"),
                                     ACT.Sigmoid).then_inc(g_free[b % 2], 1)

            queries(0)
            sub_scores(0)
            queries(1)
            gate_exp(0)
            sub_scores(1)
            expert_gelu(0)
            gate_exp(1)
            embed(0)
            expert_gelu(1)
            embed(1)

        @block.tensor
        def _(pe):
            def unit(u):
                pe.wait_ge(ring_full[u % RING], 16 * (u // RING + 1))

            def block_free(b):
                if b >= 2:
                    pe.wait_ge(g_free[b % 2], b // 2)

            def cols(b, slot, xT, k0=0, first=True, last=True):
                w = ring[:, slot, :].rearrange("p (k n) -> p k n", k=DC)
                for t in range(TT):
                    for k in range(DC):
                        ins = nc.tensor.matmul(G[:, b % 2, t, :], xT[:, k0 + k, t * P:(t + 1) * P], w[:, k, :],
                                               start=(first and k == 0), stop=(last and k == DC - 1))
                return ins

            def rows(b, slot, xT):
                w = ring[:, slot, :].rearrange("p (k n) -> p k n", k=DC)
                for c in range(4):
                    for k in range(DC):
                        ins = nc.tensor.matmul(G[:, b % 2, c // 2, (c % 2) * TOK:(c % 2 + 1) * TOK],
                                               w[:, k, c * P:(c + 1) * P], xT[:, k, :],
                                               start=(k == 0), stop=(k == DC - 1))
                return ins

            def simple(kind, xT, name, n=None, u0=0):
                for i in range(u0, u0 + (n or dict(UNITS)[name])):
                    u, b = UNIT0[name] + i, BLOCK0[name] + i
                    unit(u)
                    block_free(b)
                    kind(b, u % RING, xT).then_inc(unit_used, 1)

            def modulation(b, slot, xT):
                w = ring[:, slot, :].rearrange("p (k n) -> p k n", k=DC)
                for k in range(DC):
                    ins = nc.tensor.matmul(G[:, b % 2, 0, :], xT[:, k, :], w[:, k, :],
                                           start=(k == 0), stop=(k == DC - 1))
                return ins

            def turn(name, g, pieces):
                n = TURN0[name] + g
                if n >= 2:
                    pe.wait_ge(t_free[n % 2], n // 2)
                for s, piece in enumerate(pieces):
                    ins = piece(T[:, n % 2, s * P:(s + 1) * P])
                ins.then_inc(t_ready, 1)

            def turned(name, count):
                last = TURN0[name] + count - 1
                for n in (last, last - 1):
                    if n >= 0:
                        pe.wait_ge(t_free[n % 2], n // 2 + 1)

            def flipped(src):
                return lambda dst: nc.tensor.transpose(dst[0:src.shape[1], :], src, ident)

            def turn_stream(name, src):
                for g in range(4):
                    turn(name, g, [flipped(src[:, t, c * P:(c + 1) * P]) for c in (2 * g, 2 * g + 1) for t in range(TT)])
                turned(name, 4)

            def norm(n):
                pe.wait_ge(sem("norm_xhat"), 2 * (n + 1))
                turn_stream(f"norm{n}", ybuf)

            def spare(name, i=0):
                n = SPARE0[name] + i
                if n >= 1:
                    pe.wait_ge(m_free, n)

            pe.wait_ge(sem("l_rel"), 32)
            nc.tensor.matmul(M[0:H, 0, 0:RELS], relb[:, :], onehot[:, :], start=True, stop=True).then_inc(m_ready, 1)
            pe.wait_ge(sem("cB"), 1)
            simple(modulation, cB, "ada0a")
            pe.wait_ge(sem("l_consts"), 16)
            norm(0)
            spare("gates")
            pe.wait_ge(sem("l_wgate"), 16)
            for t in range(TT):
                for k in range(DC):
                    ins = nc.tensor.matmul(M[:, 0, 16 * t:16 * t + 16], hT[:, k, t * P:(t + 1) * P], wgate[:, k, :],
                                           start=(k == 0), stop=(k == DC - 1))
            ins.then_inc(m_ready, 1)
            simple(rows, hT, "a_qk", 1)
            spare("cum")
            pe.wait_ge(sem("logf"), 1)
            for t in range(TT):
                nc.tensor.matmul(M[:, 0, 16 * t:16 * t + 8], upper, glf[:, t, :], start=True, stop=True)
                ins = nc.tensor.matmul(M[:, 0, 16 * t + 8:16 * t + 16], ones[:, :], glf[:, t, :], start=True, stop=True)
            ins.then_inc(m_ready, 1)
            simple(rows, hT, "a_qk", 1, 1)
            for t in range(TT):
                spare("rb", t)
                pe.wait_ge(sem("diag"), t + 1)
                for g in range(2):
                    ins = nc.tensor.matmul(M[:, g, :], ones[:, :],
                                           diag[:, t, 4 * g:4 * g + 4, :].rearrange("p h n -> p (h n)"),
                                           start=True, stop=True)
                ins.then_inc(m_ready, 1)
            simple(cols, hT, "a_v")
            simple(cols, hT, "a_o")
            for i in range(2):
                read_out(pe, "a_qk", i)
            turn("k_tok", 0, [flipped(kT[:, c, 0:P]) for c in range(4)])
            for t in range(TT):
                spare("score", t)
                for h in range(H):
                    r = slice(64 * (h % 2), 64 * (h % 2) + 64)
                    ins = nc.tensor.matmul(MP[:, h % 2, h // 2, :], qT[r, h // 2, t * P:(t + 1) * P],
                                           kT[r, h // 2, t * P:(t + 1) * P], start=True, stop=True)
                ins.then_inc(m_ready, 1)
                simple(modulation, cB, ("ada0b", "ada0c")[t])
            for i in range(2):
                read_out(pe, "a_v", i)
            turned("k_tok", 1)
            spare("c_loc")
            for c in range(4):
                ins = nc.tensor.matmul(M[:, c // 2, (c % 2) * 256:(c % 2) * 256 + 256], kw[:, c * P:(c + 1) * P],
                                       vtok[:, 0, 2 * c:2 * c + 2, :].rearrange("p h e -> p (h e)"),
                                       start=True, stop=True)
            ins.then_inc(m_ready, 1)
            turn("n_loc", 0, [(lambda dst, c=c: nc.tensor.matmul(dst[:, 0:1], kw[:, c * P:(c + 1) * P], ones[:, 0:1],
                                                                 start=True, stop=True)) for c in range(4)])
            for t in range(TT):
                pe.wait_ge(m_free, SPARE0["score"] + t + 1)
                for g in range(2):
                    turn("scoreT", 2 * t + g, [flipped(dec[:, t, 4 * g + s, :]) for s in range(4)])

            def pv(t):
                spare(f"pv{t}")
                for n in (TURN0["scoreT"] + 2 * t, TURN0["scoreT"] + 2 * t + 1):
                    pe.wait_ge(t_free[n % 2], n // 2 + 1)
                for h in range(H):
                    ins = nc.tensor.matmul(M8[:, h, :], decT[:, t, h, :], vtok[:, t, h, :], start=True, stop=True)
                ins.then_inc(m_ready, 1)

            simple(modulation, cB, "ada0d")
            pv(0)
            spare("qc")
            for c in range(4):
                ins = nc.tensor.matmul(M[:, c // 2, (c % 2) * 256:(c % 2) * 256 + 256], qT[:, c, P:2 * P], cbd[:, c, :],
                                       start=True, stop=True)
            ins.then_inc(m_ready, 1)
            turned("n_loc", 1)
            turn("qn", 0, [(lambda dst, c=c: nc.tensor.matmul(dst[:, 0:2], qT[:, c, P:2 * P], nbd[:, c, :],
                                                              start=True, stop=True)) for c in range(4)])
            pv(1)
            simple(modulation, cB, "ada0e")
            pe.wait_ge(sem("mixed_a"), 2)
            turn_stream("mix_a", ybuf)
            simple(cols, hT, "a_out")
            simple(modulation, cB, "ada1a")

            def ffn(f):
                u0, b0 = UNIT0[f"up{f}"], BLOCK0[f"up{f}"]
                with pe.Fori(0, 2) as i:
                    for j in range(RING):
                        pe.wait_ge(ring_full[j], 16 * i + 16 * (u0 // RING + 1))
                        pe.wait_ge(g_free[j % 2], 2 * i + (b0 + j) // 2)
                        rows(j, j, hT).then_inc(unit_used, 1)
                pe.wait_ge(sem("relu_free"), 8 * (f + 1) + 2)
                u0, b0 = UNIT0[f"down{f}"], BLOCK0[f"down{f}"]
                for nb in range(2):
                    block_free(b0 + nb)
                    for g in range(4):
                        u = u0 + 4 * nb + g
                        unit(u)
                        cols(b0 + nb, u % RING, fT, DC * g, g == 0, g == 3).then_inc(unit_used, 1)

            norm(1)
            ffn(0)
            simple(modulation, cB, "ada1b")
            norm(2)
            simple(rows, hT, "b_u")
            simple(cols, hT, "b_v")
            simple(modulation, cB, "ada1c")
            pe.wait_ge(sem("ws_masked"), 1)
            for t in range(TT):
                pe.wait_ge(sem("v_normed"), t + 1)
                for r in range(2):
                    spare("sv", 2 * t + r)
                    for j in range(8):
                        g = 8 * r + j
                        ins = nc.tensor.matmul(M8[:, j, :], vsg[:, t, g * P:(g + 1) * P], wsT[:, g, :],
                                               start=True, stop=True)
                    ins.then_inc(m_ready, 1)
            pe.wait_ge(sem("gated"), 4)
            for nb in range(2):
                b = BLOCK0["b_out"] + nb
                block_free(b)
                for g in range(2):
                    u = UNIT0["b_out"] + 2 * nb + g
                    unit(u)
                    cols(b, u % RING, uT, DC * g, g == 0, g == 1).then_inc(unit_used, 1)
            norm(3)
            ffn(1)
            norm(4)
            spare("kiwi")
            pe.wait_ge(sem("l_kiwi"), 16)
            for k in range(DC):
                nc.tensor.matmul(M[:, 0, 0:TOK], wkiwi[:, k, 0:2 * AH], hT[:, k, :], start=(k == 0), stop=(k == DC - 1))
            for t in range(TT):
                for k in range(DC):
                    ins = nc.tensor.matmul(M[:, 1, H * t:H * t + H], hT[:, k, t * P:(t + 1) * P],
                                           wkiwi[:, k, 2 * AH:], start=(k == 0), stop=(k == DC - 1))
            ins.then_inc(m_ready, 1)
            simple(rows, hT, "qi")
            simple(cols, hT, "qkv")
            pe.wait_ge(m_free, SPARE0["kiwi"] + 1)
            read_out(pe, "qi", 0)
            for i, (t, h0, nh) in enumerate(((0, 0, 8), (1, 0, 4), (1, 4, 4))):
                spare("dots", i)
                keys = P * (t + 1)
                for h in range(h0, h0 + nh):
                    r = slice(64 * (h % 2), 64 * (h % 2) + 64)
                    s = (h - h0) // 2
                    ins = nc.tensor.matmul(M[:, h % 2, s * keys:(s + 1) * keys], qiT[r, h // 2, t * P:(t + 1) * P],
                                           kiT[r, 0:keys], start=True, stop=True)
                ins.then_inc(m_ready, 1)
            simple(rows, hT, "glu")
            for a, (name, src) in enumerate((("qT", qtok), ("kT", ktok))):
                pe.wait_ge(sem("qk_normed"), a + 1)
                for g in range(2):
                    turn(name, g, [flipped(src[:, t, c * P:(c + 1) * P]) for c in (2 * g, 2 * g + 1) for t in range(TT)])
            simple(cols, hT, "gates")
            turned("qT", 2)
            turned("kT", 2)
            pe.wait_ge(sem("l_relh"), 16)

            def logits(i, t, h0, nh):
                spare("logit", i)
                keys = P * (t + 1)
                for h in range(h0, h0 + nh):
                    r = slice(64 * (h % 2), 64 * (h % 2) + 64)
                    s = (h - h0) // 2
                    dst = M[:, h % 2, s * keys:(s + 1) * keys]
                    nc.tensor.matmul(dst, q2T[r, h // 2, t * P:(t + 1) * P], k2T[r, h // 2, 0:keys],
                                     start=True, stop=False)
                    ins = nc.tensor.matmul(dst, flip, relH[:, h, P - P * t:P - P * t + keys], start=False, stop=True)
                ins.then_inc(m_ready, 1)

            def probs(t, kt):
                pe.wait_ge(sem("probs_normed"), t + 1)
                for g in range(2):
                    turn("probT", 2 * (t + kt) + g,
                         [flipped(logit[:, 4 * g + s, kt * P:(kt + 1) * P]) for s in range(4)])

            logits(0, 0, 0, 8)
            probs(0, 0)
            logits(1, 1, 0, 4)
            logits(2, 1, 4, 4)
            probs(1, 0)
            probs(1, 1)
            turned("probT", 6)
            read_out(pe, "qkv", 2)
            spare("att")
            for t in range(TT):
                for h in range(H):
                    r = slice(64 * (h % 2), 64 * (h % 2) + 64)
                    for kt in range(t + 1):
                        ins = nc.tensor.matmul(M[r, t, (h // 2) * P:(h // 2 + 1) * P], vatt[:, kt, h * AH:(h + 1) * AH],
                                               prT[:, t + kt, h, :], start=(kt == 0), stop=(kt == t))
            ins.then_inc(m_ready, 1)
            pe.wait_ge(sem("tap"), CH // P * TAPS)
            for g in range(2):
                turn("conv_tok", g, [flipped(ycT[:, 2 * g + s // 2, (s % 2) * P:(s % 2 + 1) * P]) for s in range(4)])
            pe.wait_ge(sem("silu"), 1)
            for g in range(2):
                turn("convT", g, [flipped(yct[:, t, c * P:(c + 1) * P]) for c in (2 * g, 2 * g + 1) for t in range(TT)])
            pe.wait_ge(m_free, SPARE0["att"] + 1)
            for name, xT in (("att", attT), ("conv", cT)):
                if name == "conv":
                    turned("convT", 2)
                u = UNIT0[name]
                unit(u)
                w = ring[:, u % RING, :].rearrange("p (k n) -> p k n", k=4)
                for nb in range(2):
                    b = BLOCK0[name] + nb
                    block_free(b)
                    for t in range(TT):
                        for k in range(4):
                            ins = nc.tensor.matmul(G[:, b % 2, t, :], xT[:, k, t * P:(t + 1) * P],
                                                   w[:, k, nb * 512:(nb + 1) * 512], start=(k == 0), stop=(k == 3))
                    ins.then_inc(unit_used if nb else sem("half_done"), 1)
            pe.wait_ge(sem("mixed_c"), 2)
            turn_stream("mix_c", ybuf)
            simple(cols, hT, "out")
            norm(5)
            for t in range(TT):
                for i in range(2):
                    b = BLOCK0["peer_q"] + 2 * t + i
                    block_free(b)
                    for half in range(2):
                        u = UNIT0["peer_q"] + 2 * i + half
                        unit(u)
                        w = ring[:, u % RING, :].rearrange("p (k n) -> p k n", k=DC)
                        for c in range(4):
                            for k in range(DC):
                                ins = nc.tensor.matmul(G[:, b % 2, half, c * P:(c + 1) * P], w[:, k, c * P:(c + 1) * P],
                                                       hT[:, k, t * P:(t + 1) * P], start=(k == 0), stop=(k == DC - 1))
                        if t == 1:
                            ins.then_inc(unit_used, 1)
                    if t == 0:
                        ins.then_inc(sem("tile0_queries"), 1)
                if t == 0:
                    pe.wait_ge(sem("l_sk"), 16)
                for i in range(2):
                    read_out(pe, "peer_q", 2 * t + i)
                for r in range(2):
                    spare("psc", 2 * t + r)
                    for j in range(H):
                        ins = nc.tensor.matmul(M8[:, j, :], pqT[:, H * r + j, t * P:(t + 1) * P], skT[:, H * r + j, :],
                                               start=True, stop=True)
                    ins.then_inc(m_ready, 1)
            pe.wait_ge(sem("l_pt"), 16)
            pe.wait_ge(sem("l_proj"), 16)
            for t in range(TT):
                b = BLOCK0["ple"] + 2 * t
                block_free(b)
                for nb in range(2):
                    for k in range(2):
                        ins = nc.tensor.matmul(G[:, b % 2, nb, :], ptT[:, k, t * P:(t + 1) * P],
                                               wproj[:, k, nb * 512:(nb + 1) * 512], start=(k == 0), stop=(k == 1))
                ins.then_inc(sem("proj_done"), 1)
                pe.wait_ge(sem("norm_xhat"), 13 + t)
                for g in range(2):
                    turn("norm6", 2 * t + g, [flipped(ybuf[:, t, c * P:(c + 1) * P]) for c in range(4 * g, 4 * g + 4)])
                turned("norm6", 2 * t + 2)
                b += 1
                block_free(b)
                for nb in range(2):
                    u = UNIT0["ple"] + nb
                    unit(u)
                    w = ring[:, u % RING, :].rearrange("p (k n) -> p k n", k=DC)
                    for k in range(DC):
                        ins = nc.tensor.matmul(G[:, b % 2, nb, :], hT[:, k, t * P:(t + 1) * P], w[:, k, :],
                                               start=(k == 0), stop=(k == DC - 1))
                ins.then_inc(sem("ple_gate"), 1)

        @block.vector
        def _(dve):
            V = nc.vector
            n_dve = [0]

            def link(ins):
                n_dve[0] += 1
                ins.then_inc(sem("dve_step"), 1)
                dve.wait_ge(sem("dve_step"), n_dve[0])

            def turn_done(name, g):
                n = TURN0[name] + g
                dve.wait_ge(t_ready, n + 1)
                return n % 2

            def spare_done(name, i=0):
                dve.wait_ge(m_ready, SPARE0[name] + i + 1)

            def spare_read(ins, name, i=0):
                ins.then_inc(m_free, 1)
                dve.wait_ge(m_free, SPARE0[name] + i + 1)

            def block_read(ins, name, i):
                ins.then_inc(g_free[(BLOCK0[name] + i) % 2], 1)

            def copies(name, groups):
                for g, dst in enumerate(groups):
                    p = turn_done(name, g)
                    V.tensor_copy(dst, T[:, p, :]).then_inc(t_free[p], 1)

            def modulations(name):
                l, first = ADA[name]
                dve.wait_ge(sem(f"l_mod{l}"), 16)
                for i in range(dict(UNITS)[name]):
                    b = block_done(dve, name, i)
                    part = mod[:, l, (first + i) * 512:(first + i + 1) * 512]
                    block_read(V.tensor_tensor(part, part, G[:, b % 2, 0, :], ALU.add), name, i)
                for i in range(dict(UNITS)[name]):
                    read_out(dve, name, i)

            def column(l, m, k):
                work = carve(arena, 8192 if (l, k) < (0, 2) else 10240, (DC, P))
                link(V.tensor_tensor(work, mod[:, l, m * D:(m + 1) * D].rearrange("p (c n) -> p c n", n=P),
                                     bcast(ident, 1, DC), ALU.mult))
                link(V.tensor_reduce(mcol[:, l, k, :], work, AX_X, ALU.add))

            def scale_column(l, half):
                link(V.scalar_tensor_tensor(out=scol[:, 2 * l + half, :], in0=mcol[:, l, 2 * half + 1, :], scalar=1.0,
                                            in1=ncols[:, 2 * l + half, :], op0=ALU.add, op1=ALU.mult))

            def gain_row(l, half):
                dve.wait_ge(sem("l_rows2"), 32 * (l + 1))
                m = 3 * half + 2
                part = mod[:, l, m * D:(m + 1) * D]
                V.tensor_tensor(part, part, rows2[:, half, :], ALU.mult).then_inc(sem("gains"), 1)
                dve.wait_ge(sem("gains"), 2 * l + half + 1)

            def norm(n):
                dve.wait_ge(sem("norm_std"), n + 1)
                V.reciprocal(rstd, std).then_inc(sem("norm_rstd"), 1)
                for g in range(4):
                    p = turn_done(f"norm{n}", g)
                    for c in (2 * g, 2 * g + 1):
                        src = T[:, p, (c % 2) * TOK:(c % 2 + 1) * TOK]
                        if n < 4:
                            ins = V.tensor_scalar(hT[:, c, :], src, scol[:, n, c:c + 1],
                                                  mcol[:, n // 2, 2 * (n % 2), c:c + 1], ALU.mult, ALU.add)
                        else:
                            ins = V.tensor_scalar(hT[:, c, :], src, ncols[:, n, c:c + 1], None, ALU.mult)
                    ins.then_inc(t_free[p], 1)

            def post(p):
                l, half = p // 2, p % 2
                dve.wait_ge(sem("post_std"), p + 1)
                link(V.reciprocal(rstd, std))
                row = mod[:, l, (3 * half + 2) * D:(3 * half + 3) * D]
                for t in range(TT):
                    link(V.scalar_tensor_tensor(out=ybuf[:, t, :], in0=ybuf[:, t, :], scalar=rstd[:, t:t + 1], in1=row,
                                                op0=ALU.mult, op1=ALU.mult))
                    ins = V.tensor_tensor(xs[:, t, :], xs[:, t, :], ybuf[:, t, :], ALU.add)
                    if t == 0:
                        link(ins)
                ins.then_inc(sem("x_ready"), 1)

            def squares(f):
                u0 = BLOCK0[f"up{f}"]
                with dve.Fori(0, 2) as i:
                    for j in range(4):
                        dve.wait_ge(g_free[j % 2], 2 * i + ((u0 + j) // 2 + 1))
                        r = frelu[:, j % 2, :, :]
                        V.tensor_tensor(fT[:, bass.ds(16 * i + 4 * j, 4), :], r, r, ALU.mult).then_inc(sem("relu_free"), 1)

            V.memset(epsc, EPS).then_inc(sem("consts_set"), 1)
            V.memset(onec, 1.0).then_inc(sem("consts_set"), 1)
            V.memset(ones[:, :], 1.0).then_inc(sem("ones_set"), 1)
            for name, n in (("relu_free", 2), ("row_used", GBUF)):
                for k in range(n):
                    V.memset(mprev[:, 0, :], 0.0).then_inc(sem(name), 1)
                    dve.wait_ge(sem(name), k + 1)
            dve.wait_ge(sem("csig"), 1)
            link(V.tensor_tensor(cact, ccol, csig, ALU.mult))
            V.tensor_copy(cB[:, :, :], bcast(cact, 2, P)).then_inc(sem("cB"), 1)
            spare_done("rel")
            spare_read(V.tensor_copy(relwork[0:H, :], M[0:H, 0, 0:RELS]), "rel")
            modulations("ada0a")
            dve.wait_ge(sem("l_consts"), 16)
            dve.wait_ge(sem("l_ncols"), 16)
            column(0, 0, 0)
            column(0, 1, 1)
            scale_column(0, 0)
            norm(0)
            dve.wait_ge(sem("l_bif"), 16)
            spare_done("gates")
            spare_read(V.tensor_tensor(gin, M[:, 0, 0:32].rearrange("p (t n) -> p t n", t=TT), bcast(bif[:, :], 1, TT),
                                       ALU.add), "gates")
            dve.wait_ge(sem("gth"), 1)
            link(V.tensor_scalar(gii, gth[:, :, 0:H], CAP, None, ALU.mult))
            dve.wait_ge(sem("glf"), 1)
            V.tensor_scalar(glf, glf, -1.0, None, ALU.mult).then_inc(sem("logf"), 1)
            spare_done("cum")
            spare_read(V.tensor_copy(gcum, M[:, 0, 0:32].rearrange("p (t a n) -> p t a n", t=TT, a=2)), "cum")
            link(V.tensor_tensor(gr, gii, gcum[:, :, 0, :], ALU.subtract))
            for t in range(TT):
                V.tensor_tensor(diag[:, t, :, :], bcast(ident, 1, H), bcast(gr[:, t, :], 2, P), ALU.mult).then_inc(sem("diag"), 1)
            for t in range(TT):
                spare_done("rb", t)
                link(V.tensor_reduce(maxr[:, t, :], M8, AX_X, ALU.max))
                spare_read(V.tensor_tensor(dec[:, t, :, :], M8, bcast(causal, 1, H), ALU.add), "rb", t)
                link(V.tensor_reduce(rowm[:, t, :], dec[:, t, :, :], AX_X, ALU.max))
            link(V.scalar_tensor_tensor(out=mprev[:, 1, :], in0=maxr[:, 0, :], scalar=0.0, in1=gcum[:, 0, 1, :],
                                        op0=ALU.max, op1=ALU.add))
            link(V.tensor_tensor(mx, mprev, rowm, ALU.max))
            link(V.tensor_scalar(nmx, mx, -1.0, None, ALU.mult))
            link(V.tensor_tensor(dif, mprev, mx, ALU.subtract))
            link(V.tensor_tensor(mj, gcum[:, :, 0, :], mx, ALU.add))
            V.scalar_tensor_tensor(out=wdif, in0=maxr[:, 0, :], scalar=0.0, in1=gr[:, 0, :],
                                   op0=ALU.max, op1=ALU.subtract).then_inc(sem("mx"), 1)
            for i in range(2):
                read_out(dve, "a_o", i)
            dve.wait_ge(sem("l_hnorm"), 16)
            for t in range(TT):
                link(V.tensor_tensor(osig[:, t, :], osig[:, t, :], hnrow, ALU.mult))
            link(V.memset(cbd, 0.0))
            link(V.memset(nbd, 0.0))
            dve.wait_ge(sem("wgt"), 1)
            p = turn_done("k_tok", 0)
            V.tensor_tensor(kw.rearrange("p (h d) -> p h d", h=H), T[:, p, :].rearrange("p (h d) -> p h d", h=H),
                            bcast(wgt, 2, DK), ALU.mult).then_inc(t_free[p], 1)
            for t in range(TT):
                spare_done("score", t)
                dve.wait_ge(sem("decay"), H * (t + 1))
                d = par(dec[:, t, :, :])
                spare_read(V.tensor_tensor(d, MP, d, ALU.mult), "score", t)
                link(V.tensor_reduce(rsum[:, t, :], dec[:, t, :, :], AX_X, ALU.add))
                modulations(("ada0b", "ada0c")[t])
            spare_done("c_loc")
            m4 = M[:, :, :].rearrange("p b (c n) -> p (b c) n", n=2 * DV)
            link(V.tensor_copy(cbd[0:DK, :, 0:DV], m4[0:DK, :, 0:DV]))
            spare_read(V.tensor_copy(cbd[DK:P, :, DV:], m4[DK:P, :, DV:]), "c_loc")
            p = turn_done("n_loc", 0)
            t4 = T[:, p, :].rearrange("p (c n) -> p c n", c=4)
            link(V.tensor_copy(nbd[0:DK, :, 0:1], t4[0:DK, :, 0:1]))
            V.tensor_copy(nbd[DK:P, :, 1:2], t4[DK:P, :, 0:1]).then_inc(t_free[p], 1)
            copies("scoreT", [decT[:, t, 4 * g:4 * g + 4, :].rearrange("p h n -> p (h n)") for t in range(TT) for g in range(2)])
            modulations("ada0d")
            spare_done("pv0")
            spare_read(V.tensor_copy(dec[:, 0, :, :], M8), "pv0")
            dve.wait_ge(sem("rel_out"), 16)
            spare_done("qc")
            spare_read(V.tensor_tensor(qc, M8, bcast(einter[:, 1, :], 2, DV), ALU.mult), "qc")
            p = turn_done("qn", 0)
            V.tensor_copy(qnv.rearrange("p (c n) -> p c n", c=4),
                          T[:, p, :].rearrange("p (c n) -> p c n", c=4)[:, :, 0:2]).then_inc(t_free[p], 1)
            dve.wait_ge(t_free[p], (TURN0["qn"] // 2) + 1)
            spare_done("pv1")
            spare_read(V.tensor_tensor(dec[:, 1, :, :], M8, qc, ALU.add), "pv1")
            modulations("ada0e")
            link(V.tensor_copy(den[:, 0, :], rsum[:, 0, :]))
            link(V.tensor_tensor(den[:, 1, :], qnv, einter[:, 1, :], ALU.mult))
            link(V.tensor_tensor(den[:, 1, :], den[:, 1, :], rsum[:, 1, :], ALU.add))
            link(V.scalar_tensor_tensor(out=dabs, in0=den, scalar=-1.0, in1=den, op0=ALU.mult, op1=ALU.max))
            link(V.tensor_tensor(dabs, dabs, enm, ALU.max))
            link(V.reciprocal(dinv, dabs))
            link(V.tensor_tensor(dabs, dinv, dinv, ALU.mult))
            for t in range(TT):
                link(V.tensor_tensor(decT[:, t, :, :], dec[:, t, :, :], dec[:, t, :, :], ALU.mult))
                link(V.tensor_reduce(ssn[:, t, :], decT[:, t, :, :], AX_X, ALU.add))
                V.scalar_tensor_tensor(out=ssd[:, t, :], in0=ssn[:, t, :], scalar=1.0 / DV, in1=dabs[:, t, :],
                                       op0=ALU.mult, op1=ALU.mult).then_inc(sem("ssd"), 1)
            for t in range(TT):
                dve.wait_ge(sem("hroot"), t + 1)
                link(V.reciprocal(hfac[:, t, :], hroot[:, t, :]))
                link(V.tensor_tensor(hfac[:, t, :], hfac[:, t, :], dinv[:, t, :], ALU.mult))
                link(V.tensor_tensor(dec[:, t, :, :], dec[:, t, :, :], bcast(hfac[:, t, :], 2, DV), ALU.mult))
                V.tensor_tensor(ybuf[:, t, :], dec[:, t, :, :].rearrange("p h n -> p (h n)"), osig[:, t, :],
                                ALU.mult).then_inc(sem("mixed_a"), 1)
            turned4 = [hT[:, 2 * g:2 * g + 2, :].rearrange("p c n -> p (c n)") for g in range(4)]
            copies("mix_a", turned4)
            column(0, 3, 2)
            column(0, 4, 3)
            scale_column(0, 1)
            gain_row(0, 0)
            gain_row(0, 1)
            modulations("ada1a")
            post(0)
            norm(1)
            squares(0)
            modulations("ada1b")
            column(1, 0, 0)
            column(1, 1, 1)
            scale_column(1, 0)
            post(1)
            norm(2)
            dve.wait_ge(sem("l_ws"), 16)
            V.tensor_tensor(wsT, wsT, bcast(upper, 1, GG), ALU.mult).then_inc(sem("ws_masked"), 1)
            dve.wait_ge(sem("l_bv"), 16)
            for nb in range(4):
                b = block_done(dve, "b_v", nb)
                block_read(V.tensor_tensor(vsg[:, :, nb * 512:(nb + 1) * 512], G[:, b % 2, :, :],
                                           bcast(bvrow[:, nb * 512:(nb + 1) * 512], 1, TT), ALU.add), "b_v", nb)
            modulations("ada1c")
            dve.wait_ge(sem("v_gelu"), 4)
            dve.wait_ge(sem("l_sgu"), 48)
            for t in range(TT):
                for q in range(4):
                    link(V.bn_stats(bst[:, q, :], vsg[:, t, q * 512:(q + 1) * 512]))
                V.bn_aggr(mv[:, t, :], bst).then_inc(sem("ln_var"), 1)
                dve.wait_ge(sem("ln_std"), t + 1)
                link(V.reciprocal(lnr[:, t:t + 1], lnstd[:, t:t + 1]))
                v = vsg[:, t, :]
                link(V.tensor_scalar(v, v, mv[:, t, 0:1], lnr[:, t:t + 1], ALU.subtract, ALU.mult))
                link(V.tensor_tensor(v, v, lng, ALU.mult))
                V.tensor_tensor(v, v, lnb, ALU.add).then_inc(sem("v_normed"), 1)
            for i in range(4):
                read_out(dve, "b_u", i)
            for t in range(TT):
                for r in range(2):
                    spare_done("sv", 2 * t + r)
                    spare_read(V.tensor_tensor(svb, M8, bsrow[:, 8 * r:8 * r + 8, :], ALU.add), "sv", 2 * t + r)
                    u = uT[:, 8 * r:8 * r + 8, t * P:(t + 1) * P]
                    V.tensor_tensor(u, u, svb, ALU.mult).then_inc(sem("gated"), 1)
                    dve.wait_ge(sem("gated"), 2 * t + r + 1)
            column(1, 3, 2)
            column(1, 4, 3)
            scale_column(1, 1)
            gain_row(1, 0)
            gain_row(1, 1)
            post(2)
            norm(3)
            squares(1)
            post(3)
            norm(4)
            spare_done("kiwi")
            link(V.tensor_copy(kiT, M[:, 0, 0:TOK]))
            spare_read(V.tensor_copy(wi, M[:, 1, 0:2 * H].rearrange("p (t h) -> p t h", t=TT)), "kiwi")
            rel0 = rel8.rearrange("p a (b s) -> p (a b) s", s=P)

            def add_head(t, h, dot):
                sc = score[:, t, 0:P * (t + 1)]
                if h == 0:
                    return V.tensor_scalar(sc, dot, wi[:, t, h:h + 1], None, ALU.mult)
                return V.scalar_tensor_tensor(out=sc, in0=dot, scalar=wi[:, t, h:h + 1], in1=sc, op0=ALU.mult, op1=ALU.add)

            for i, (t, h0, nh) in enumerate(((0, 0, 8), (1, 0, 4), (1, 4, 4))):
                dve.wait_ge(m_free, SPARE0["dots"] + i + 1)
                for h in range(nh):
                    src = rel0 if t == 0 else rel8
                    ins = add_head(t, h0 + h, src[:, (h % 2) * (nh // 2) + h // 2, :])
                    if h < nh - 1:
                        link(ins)
                ins.then_inc(sem("dots_done"), 1)
                dve.wait_ge(sem("dots_done"), i + 1)
            for a, (src, gain) in enumerate(((qtok, qgain), (ktok, kgain))):
                read_out(dve, "qkv", a)
                link(V.tensor_tensor(qsq, src, src, ALU.mult))
                V.tensor_reduce(qss[:, a, :, :], qsq.rearrange("p t (h d) -> p t h d", h=H), AX_X, ALU.add).then_inc(sem("qss"), 1)
                dve.wait_ge(sem("qss"), a + 1)
            dve.wait_ge(sem("l_small"), 80)
            for a, (src, gain) in enumerate(((qtok, qgain), (ktok, kgain))):
                dve.wait_ge(sem("qroot"), a + 1)
                link(V.reciprocal(qrec[:, a, :, :], qroot[:, a, :, :]))
                if a == 0:
                    link(V.tensor_scalar(qrec[:, a, :, :], qrec[:, a, :, :], AH ** -0.5, None, ALU.mult))
                v = src.rearrange("p t (h d) -> p (t h) d", h=H)
                link(V.tensor_tensor(v, v, bcast(qrec[:, a, :, :].rearrange("p t h -> p (t h)"), 2, AH), ALU.mult))
                V.tensor_tensor(v, v, bcast(gain, 1, TT * H), ALU.mult).then_inc(sem("qk_normed"), 1)
            for i in range(2):
                read_out(dve, "glu", i)
            link(V.memset(upad[:, :, 0:TAPS - 1], 0.0))
            V.tensor_tensor(upad[:, :, TAPS - 1:], aT, rel8, ALU.mult).then_inc(sem("glu_done"), 1)
            dve.wait_ge(sem("glu_done"), 1)
            copies("qT", [q2T[:, 2 * g:2 * g + 2, :].rearrange("p c n -> p (c n)") for g in range(2)])
            copies("kT", [k2T[:, 2 * g:2 * g + 2, :].rearrange("p c n -> p (c n)") for g in range(2)])
            for t in range(TT):
                sc = score[:, t, 0:P * (t + 1)]
                link(V.scalar_tensor_tensor(out=sc, in0=sc, scalar=AH ** -0.5 * H ** -0.5, in1=visible[t],
                                            op0=ALU.mult, op1=ALU.add))
                for _ in range(TOPK // 8):
                    link(V.max(top8, sc))
                    link(V.match_replace(sc, top8, sc, TAKEN))
                link(V.tensor_scalar(sc, sc, TAKEN / 2, NEG, ALU.is_gt, ALU.mult))
            dve.wait_ge(sem("l_bgate"), 16)

            def gate_bias(nb):
                b = block_done(dve, "gates", nb)
                block_read(V.tensor_tensor(gates[:, :, nb * 512:(nb + 1) * 512], G[:, b % 2, :, :],
                                           bcast(bgrow[:, nb * 512:(nb + 1) * 512], 1, TT), ALU.add), "gates", nb)

            for c0 in (0, 2):
                for w in range(TAPS):
                    for c in (c0, c0 + 1):
                        src = upad[:, c, w:w + TOK]
                        if w == 0:
                            ins = V.tensor_scalar(ycT[:, c, :], src, cwcol[:, c, 0:1], cbcol[:, c:c + 1], ALU.mult, ALU.add)
                        else:
                            dve.wait_ge(sem("tap"), (c0 // 2) * 2 * TAPS + 2 * w + c - c0 - 1)
                            ins = V.scalar_tensor_tensor(out=ycT[:, c, :], in0=src, scalar=cwcol[:, c, w:w + 1],
                                                         in1=ycT[:, c, :], op0=ALU.mult, op1=ALU.add)
                        ins.then_inc(sem("tap"), 1)
                gate_bias(c0)
                gate_bias(c0 + 1)

            def softmax(t):
                v = logit[:, :, 0:P * (t + 1)]
                link(V.tensor_reduce(lmax[:, t, :], v, AX_X, ALU.max))
                V.tensor_scalar(lneg[:, t, :], lmax[:, t, :], -1.0, None, ALU.mult).then_inc(sem("lneg"), 1)
                dve.wait_ge(sem("probs"), H * (t + 1))
                link(V.reciprocal(lrec[:, t, :], lsum[:, t, :]))
                V.tensor_tensor(v, v, bcast(lrec[:, t, :], 2, P * (t + 1)), ALU.mult).then_inc(sem("probs_normed"), 1)

            spare_done("logit")
            spare_read(V.tensor_tensor(par(logit[:, :, 0:P]), MP, bcast(bcast(score[:, 0, 0:P], 1, 4), 1, 2), ALU.add), "logit")
            softmax(0)
            for g in range(2):
                p = turn_done("probT", g)
                V.tensor_copy(prT[:, 0, 4 * g:4 * g + 4, :].rearrange("p h n -> p (h n)"), T[:, p, :]).then_inc(t_free[p], 1)
            for r in range(2):
                spare_done("logit", 1 + r)
                spare_read(V.tensor_tensor(par(logit[:, 4 * r:4 * r + 4, :]), M[:, :, :].rearrange("p b (j n) -> p b j n", n=TOK),
                                           bcast(bcast(score[:, 1, :], 1, 2), 1, 2), ALU.add), "logit", 1 + r)
            softmax(1)
            for g in range(2, 6):
                p = turn_done("probT", g)
                V.tensor_copy(prT[:, g // 2, 4 * (g % 2):4 * (g % 2) + 4, :].rearrange("p h n -> p (h n)"),
                              T[:, p, :]).then_inc(t_free[p], 1)
            spare_done("att")
            spare_read(V.tensor_copy(attT.rearrange("p c (t n) -> p t c n", t=TT), MP), "att")
            for g in range(2):
                p = turn_done("conv_tok", g)
                V.tensor_copy(yct[:, :, 2 * g * P:(2 * g + 2) * P].rearrange("p t (c n) -> p t c n", c=2),
                              T[:, p, :].rearrange("p (c t n) -> p t c n", c=2, t=TT)).then_inc(t_free[p], 1)
            for g in range(2):
                n = TURN0["conv_tok"] + g
                dve.wait_ge(t_free[n % 2], n // 2 + 1)
            dve.wait_ge(sem("l_cln"), 32)
            for t in range(TT):
                v = yct[:, t, :]
                link(V.bn_stats(bst[:, 0, :], v))
                V.bn_aggr(mv[:, t, :], bst[:, 0:1, :]).then_inc(sem("cln_var"), 1)
                dve.wait_ge(sem("cln_std"), t + 1)
                link(V.reciprocal(lnr[:, t:t + 1], lnstd[:, t:t + 1]))
                link(V.tensor_scalar(v, v, mv[:, t, 0:1], lnr[:, t:t + 1], ALU.subtract, ALU.mult))
                link(V.tensor_tensor(v, v, clng, ALU.mult))
                V.tensor_tensor(v, v, clnb, ALU.add).then_inc(sem("cln"), 1)
            dve.wait_ge(sem("ysg"), 1)
            V.tensor_tensor(yct, yct, ysg, ALU.mult).then_inc(sem("silu"), 1)
            copies("convT", [cT[:, 2 * g:2 * g + 2, :].rearrange("p c n -> p (c n)") for g in range(2)])
            dve.wait_ge(sem("gate_sig"), 4)
            for nb in range(2):
                b = block_done(dve, "att", nb)
                block_read(V.tensor_tensor(ybuf[:, :, nb * 512:(nb + 1) * 512], G[:, b % 2, :, :],
                                           gates[:, :, nb * 512:(nb + 1) * 512], ALU.mult), "att", nb)
            for nb in range(2):
                b = block_done(dve, "conv", nb)
                g = gates[:, :, D + nb * 512:D + (nb + 1) * 512]
                block_read(V.tensor_tensor(g, G[:, b % 2, :, :], g, ALU.mult), "conv", nb)
            for i in range(2):
                read_out(dve, "conv", i)
            for nb in range(2):
                y = ybuf[:, :, nb * 512:(nb + 1) * 512]
                V.tensor_tensor(y, y, gates[:, :, D + nb * 512:D + (nb + 1) * 512], ALU.add).then_inc(sem("mixed_c"), 1)
            copies("mix_c", turned4)
            for nb in range(2):
                b = block_done(dve, "out", nb)
                x = xs[:, :, nb * 512:(nb + 1) * 512]
                block_read(V.tensor_tensor(x, x, G[:, b % 2, :, :], ALU.add), "out", nb)
            norm(5)
            dve.wait_ge(sem("l_fg"), 16)
            for t in range(TT):
                link(V.tensor_tensor(h2[:, t, :], ybuf[:, t, :], fgrow, ALU.mult))

            def top16(rows):
                start, per = n_dve[0], len(rows)
                for step in range(5):
                    for j, (vals, idx, src) in enumerate(rows):
                        if step:
                            dve.wait_ge(sem("dve_step"), start + (step - 1) * per + j + 1)
                        e = slice(8 * (step // 3), 8 * (step // 3) + 8)
                        if step in (0, 3):
                            ins = V.max(vals[:, e], src)
                        elif step in (1, 4):
                            ins = V.max_index(idx[:, e], vals[:, e], src)
                        else:
                            ins = V.match_replace(src, vals[:, 0:8], src, TAKEN)
                        ins.then_inc(sem("dve_step"), 1)
                        n_dve[0] += 1
                dve.wait_ge(sem("dve_step"), n_dve[0])

            def key_top(r0, n):
                top16([(sv[:, r // 2, r % 2, :], siu[:, r // 2, r % 2, :], psc[:, r, :]) for r in range(r0, r0 + n)])

            def pair_top(h0, n):
                top16([(topv[:, h, :], tju[:, 0, h, :], cand[:, h, :, :].rearrange("p a b -> p (a b)"))
                       for h in range(h0, h0 + n)])

            def pairs():
                link(V.tensor_copy(sif, siu))
                link(V.tensor_tensor(cand, bcast(sv[:, :, 0, :], 3, PK), bcast(sv[:, :, 1, :], 2, PK), ALU.add))

            def choose(t):
                link(V.tensor_copy(gmax, topv[:, :, 0]))
                V.tensor_tensor(topv, topv, bcast(gmax, 2, PK), ALU.subtract).then_inc(sem("topv"), 1)
                link(V.tensor_scalar(tju[:, 1, :, :], tju[:, 0, :, :], 4, None, ALU.logical_shift_right))
                link(V.tensor_scalar(tju[:, 2, :, :], tju[:, 0, :, :], PK - 1, None, ALU.bitwise_and))
                link(V.tensor_copy(tjf, tju[:, 1:3, :, :]))
                for c in range(2):
                    link(V.tensor_tensor(cand, bcast(tjf[:, c, :, :], 3, PK), bcast(bcast(iota16, 1, PK), 1, H), ALU.is_equal))
                    link(V.tensor_tensor(eqc, cand, bcast(sif[:, :, c, :], 2, PK), ALU.mult))
                    link(V.tensor_reduce(i12[:, c, :, :], eqc, AX_X, ALU.add))
                V.scalar_tensor_tensor(out=eidx[:, t, :], in0=i12[:, 0, :, :].rearrange("p h k -> p (h k)"),
                                       scalar=float(NKEYS), in1=i12[:, 1, :, :].rearrange("p h k -> p (h k)"),
                                       op0=ALU.mult, op1=ALU.add).then_inc(sem("eidx_ready"), 1)
                dve.wait_ge(sem("gate_exp"), t + 1)
                link(V.tensor_reduce(gsum, topv, AX_X, ALU.add))
                link(V.reciprocal(grec, gsum))
                link(V.tensor_tensor(gateT[:, t, :].rearrange("p (h k) -> p h k", h=H), topv, bcast(grec, 2, PK), ALU.mult))

            def expert_dots(t):
                def between(i):
                    for j in range(GBUF):
                        row = gbufs[j // 4][:, j % 4, :]
                        dve.wait_ge(sem(f"row{j}"), 16 * i + 16 * (2 * t * NSEL // GBUF + 1))
                        V.scalar_tensor_tensor(out=row, in0=row, scalar=1.0, in1=h2[:, t, :], op0=ALU.mult, op1=ALU.mult,
                                               accum_out=dots[:, t, bass.ds(GBUF * i + j, 1)]).then_inc(sem("row_used"), 1)
                return between

            def expert_sums(t):
                base = (2 * t + 1) * NSEL

                def between(i):
                    for j in range(GBUF):
                        dve.wait_ge(sem(f"row{j}"), 16 * i + 16 * (base // GBUF + 1))
                        dve.wait_ge(sem("row_used"), GBUF * i + (base + j + GBUF))
                        V.scalar_tensor_tensor(out=xs[:, t, :], in0=gbufs[j // 4][:, j % 4, :],
                                               scalar=actv[:, t, bass.ds(GBUF * i + j, 1)],
                                               in1=xs[:, t, :], op0=ALU.mult, op1=ALU.add).then_inc(sem("row_used"), 1)
                return between

            def weights_of(t):
                dve.wait_ge(sem("row_used"), (2 * t + 1) * NSEL + GBUF)
                V.memset(gmax, 0.0).then_inc(sem("dots_all"), 1)
                dve.wait_ge(sem("gelu"), t + 1)
                link(V.tensor_tensor(actv[:, t, :], actv[:, t, :], gateT[:, t, :], ALU.mult))

            def experts(uses, i0, i1):
                with dve.Fori(i0, i1) as i:
                    uses(i)

            rounds = NSEL // GBUF
            dve.wait_ge(m_free, SPARE0["psc"] + 2)
            for r0 in range(0, HC, 4):
                key_top(r0, 4)
            pairs()
            for h0 in range(0, H, 4):
                pair_top(h0, 4)
            choose(0)
            dve.wait_ge(m_free, SPARE0["psc"] + 4)
            for r0 in range(0, HC, 2):
                key_top(r0, 2)
                experts(expert_dots(0), r0 * rounds // HC, (r0 + 2) * rounds // HC)
            weights_of(0)
            pairs()
            for h0 in range(0, H, 2):
                pair_top(h0, 2)
                experts(expert_sums(0), h0, h0 + 2)
            choose(1)
            experts(expert_sums(0), H, rounds)
            dve.wait_ge(sem("row_used"), 2 * NSEL + GBUF)
            V.memset(gmax, 0.0).then_inc(sem("x_ready"), 1)

            def embed_norm(t):
                dve.wait_ge(sem("norm_std"), 7 + t)
                V.reciprocal(rstd[:, t:t + 1], std[:, t:t + 1]).then_inc(sem("norm_rstd"), 1)

            def embed_turned(t):
                for g in range(2):
                    p = turn_done("norm6", 2 * t + g)
                    c = slice(4 * g, 4 * g + 4)
                    V.tensor_tensor(hT[:, c, t * P:(t + 1) * P], T[:, p, :].rearrange("p (c n) -> p c n", c=4),
                                    bcast(ncols[:, 6, c], 2, P), ALU.mult).then_inc(t_free[p], 1)

            def embed_add(t):
                b = block_done(dve, "ple", 2 * t)
                read_out(dve, "ple", 2 * t + 1)
                g = sig[:, t, :].rearrange("p (a n) -> p a n", a=2)
                block_read(V.tensor_tensor(g, G[:, b % 2, :, :], g, ALU.mult), "ple", 2 * t)
                read_out(dve, "ple", 2 * t)
                V.tensor_tensor(xs[:, t, :], xs[:, t, :], sig[:, t, :], ALU.add).then_inc(sem("out_done"), 1)

            experts(expert_dots(1), 0, 2)
            embed_norm(0)
            experts(expert_dots(1), 2, 4)
            embed_turned(0)
            experts(expert_dots(1), 4, 8)
            embed_add(0)
            experts(expert_dots(1), 8, rounds)
            weights_of(1)
            experts(expert_sums(1), 0, rounds)
            dve.wait_ge(sem("row_used"), 4 * NSEL + GBUF)
            V.memset(gmax, 0.0).then_inc(sem("x_ready"), 1)
            embed_norm(1)
            embed_turned(1)
            embed_add(1)


def kernel(**inputs):
    import numpy as np
    import concourse.bacc as bacc
    from concourse.bass_utils import run_bass_kernel_spmd

    v = {k: np.asarray(a) for k, a in inputs.items()}

    def chunks(w):
        return w.reshape(-1, P, w.shape[1]).transpose(1, 0, 2).reshape(P, -1)

    def col(a):
        return np.ascontiguousarray(np.moveaxis(a.reshape(a.shape[:-1] + (-1, P)), -1, 0))

    def by_cols(w, c0, n):
        return [w[:, c0 + 512 * i:c0 + 512 * (i + 1)] for i in range(n)]

    def down(w):
        return [w[D * g:D * (g + 1), 512 * nb:512 * (nb + 1)] for nb in range(2) for g in range(w.shape[0] // D)]

    wa, wb, wc = v["a_w_in"][0], v["b_w_in"][0], v["w_in_2"][0]
    ada = {name: by_cols(v["ada_w"][l], 512 * first, dict(UNITS)[name]) for name, (l, first) in ADA.items()}
    weights = {
        **ada, "a_qk": by_cols(wa, 0, 2), "a_v": by_cols(wa, 1024, 2), "a_o": by_cols(wa, 2048, 2),
        "a_out": by_cols(v["a_w_out"][0], 0, 2),
        "up0": by_cols(v["ffn_w1"][0], 0, 8), "down0": down(v["ffn_w2"][0]),
        "up1": by_cols(v["ffn_w1"][1], 0, 8), "down1": down(v["ffn_w2"][1]),
        "b_u": by_cols(wb, 0, 4), "b_v": by_cols(wb, GH, 4), "b_out": down(v["b_w_out"][0]),
        "qkv": by_cols(wc, 0, 3), "qi": by_cols(wc, 1536, 1), "glu": by_cols(wc, 2120, 2),
        "gates": by_cols(wc, 3144, 4), "att": [v["w_att_out_2"][0]], "conv": [v["w_conv_out_2"][0]],
        "out": by_cols(v["w_out_2"][0], 0, 2), "peer_q": by_cols(v["w_peer_q_2"][0], 0, 4),
        "ple": by_cols(v["w_ple_gate_2"][0], 0, 2),
    }
    ki, wi = wc[:, 2048:2112], wc[:, 2112:2120]

    p = np.arange(P)
    seen = [np.where(np.arange(P * (t + 1))[None, :] // 64 <= (P * t + p[:, None]) // 64, 0.0, NEG) for t in range(TT)]
    consts = np.concatenate([
        np.eye(P), p[:, None] <= p[None, :], np.where(p[None, :] <= p[:, None], 0.0, NEG),
        p[:, None] + p[None, :] == P - 1, *seen, np.tile(np.arange(16), (P, 1))], axis=1).astype(np.float32)
    rel = np.arange(RELS) - 255
    far = 8 + (np.log(np.maximum(np.abs(rel), 1) / 8) / np.log(1024 / 8) * 8).astype(np.int32)
    bucket = np.where(rel > 0, 16, 0) + np.where(np.abs(rel) < 8, np.abs(rel), np.minimum(far, 15))
    onehot = (np.arange(32)[:, None] == bucket[None, :]).astype(np.float32)

    given = {
        "wpack": np.stack([chunks(w) for name, _ in UNITS for w in weights[name]]),
        "x": v["x"][0], "c": col(v["c"][0]), "norm_g": v["norm_g"],
        "ncols": col(np.stack([v["norm_g"][0, 0], v["norm_g"][0, 2], v["norm_g"][1, 0], v["norm_g"][1, 2],
                               v["attn_norm_g_2"][0], v["ffn_norm_g_2"][0], v["ple_norm_g_2"][0]])),
        "ada_b": v["ada_b"], "wgate": chunks(wa[:, 3072:3088]).reshape(P, DC, 16), "b_if": v["a_b_if"][0],
        "hnorm_g": v["a_hnorm_g"][0], "bu": col(v["b_b_in"][0, :GH]), "bv": v["b_b_in"][0, GH:],
        "ln_g": v["b_ln_g"][0], "ln_b": v["b_ln_b"][0], "wsT": v["b_ws"][0].transpose(2, 0, 1),
        "bs": v["b_bs"][0].reshape(-1), "rel_bias": v["rel_bias_2"], "onehot": onehot, "consts": consts,
        "wkiwi": chunks(np.concatenate([ki, ki, wi], axis=1)).reshape(P, DC, 2 * AH + H),
        "b_gate": v["b_gate_2"][0], "q_norm_g": v["q_norm_g_2"][0], "k_norm_g": v["k_norm_g_2"][0],
        "conv_w": np.moveaxis(v["conv_w_2"][0, :, 0, :].reshape(TAPS, CH // P, P), (2, 1, 0), (0, 1, 2)),
        "conv_b": col(v["conv_b_2"][0]), "conv_ln_g": v["conv_ln_g_2"][0], "conv_ln_b": v["conv_ln_b_2"][0],
        "ffn_norm_g": v["ffn_norm_g_2"][0],
        "skT": v["peer_sub_keys_2"][0].reshape(HC, NKEYS, P).transpose(2, 0, 1),
        "peer_u": v["peer_u_2"][0], "peer_v": v["peer_v_2"][0],
        "pT": v["p_2"][0, 0].T.reshape(2, P, TOK).transpose(1, 0, 2),
        "w_ple_proj": v["w_ple_proj_2"][0].reshape(2, P, D).transpose(1, 0, 2),
    }
    given = {k: np.ascontiguousarray(a) for k, a in given.items()}
    nc = bacc.Bacc("TRN2", target_bir_lowering=False, num_devices=1)
    A = {k: nc.dram_tensor(f"in_{k}", a.shape, F32, kind="ExternalInput").ap() for k, a in given.items()}
    out = nc.dram_tensor("out", (TOK, D), F32, kind="ExternalOutput").ap()
    build(nc, A, out)
    r = run_bass_kernel_spmd(nc, [{f"in_{k}": a for k, a in given.items()}], core_ids=[0])
    return r.results[0]["out"].reshape(1, TOK, D)
```

```python
from contextlib import ExitStack

import concourse.bass as bass
from concourse import mybir

ALU = mybir.AluOpType
ACT = mybir.ActivationFunctionType
F32 = mybir.dt.float32
F32R = mybir.dt.float32r
U32 = mybir.dt.uint32
AX_X = mybir.AxisListType.X

P = 128
TOK = 256
TT = TOK // P
D = 1024
DC = D // P
H = 8
DK, DV = 64, 128
FF = 4096
GH = 2048
GG = GH // P
AH = 64
CH = 512
TAPS = 31
TOPK = 64
HC = 2 * H
PK = 16
NSEL = H * PK
NKEYS = 128
RELS = 384
EPS = 1e-6
CAP = 15.0
NEG = -1e30
TAKEN = -3e38

RING = 4
HALF = 2048
GBUF = 8

UNITS = [("ada0a", 4), ("ada0b", 2), ("a_qk", 2), ("a_v", 2), ("a_o", 2), ("ada0c", 2), ("ada0d", 2),
         ("ada0e", 2), ("ada1a", 2), ("a_out", 2), ("ada1b", 2), ("up0", 8), ("down0", 8), ("ada1c", 2), ("b_u", 4),
         ("b_v", 4), ("ada1d", 2), ("ada1e", 2), ("b_out", 4), ("ada1f", 2), ("up1", 8), ("down1", 8), ("qi", 1),
         ("glu", 2), ("qkv", 3), ("gates", 4), ("att", 1), ("conv", 1), ("out", 2), ("peer_q", 8), ("ple", 2)]
SPLIT = ("a_qk", "a_v", "a_o", "a_out", "up0", "b_u", "b_v", "up1", "qi", "qkv", "glu", "out")
FEWER = {"down0": 2, "down1": 2, "b_out": 2, "att": 2, "conv": 2, "peer_q": 4, "ple": 4}
BLOCKS = [(name, FEWER.get(name, n)) for name, n in UNITS]
ADA = {"ada0a": (0, 0), "ada0b": (0, 4), "ada0c": (0, 6), "ada0d": (0, 8), "ada0e": (0, 10), "ada1a": (1, 0),
       "ada1b": (1, 2), "ada1c": (1, 4), "ada1d": (1, 8), "ada1e": (1, 10), "ada1f": (1, 6)}
TURNS = [("norm0", 4), ("k_tok", 1), ("n_loc", 1), ("scoreT", 4), ("qn", 1), ("mix_a", 4),
         ("norm1", 4), ("norm2", 4), ("norm3", 4), ("norm4", 4), ("qT", 2), ("kT", 2), ("probT", 6),
         ("conv_tok", 2), ("convT", 2), ("mix_c", 4), ("norm5", 4), ("norm6", 4)]
SPARES = [("rel", 1), ("gates", 1), ("cum", 1), ("rb", 2), ("score", 2), ("c_loc", 1), ("pv0", 1),
          ("qc", 1), ("pv1", 1), ("sv", 4), ("kiwi", 1), ("dots", 3), ("logit", 3), ("att", 1),
          ("psc", 4)]


def starts(table):
    out, at = {}, 0
    for name, n in table:
        out[name] = at
        at += n
    out["end"] = at
    return out


UNIT0, BLOCK0, TURN0, SPARE0 = starts(UNITS), starts(BLOCKS), starts(TURNS), starts(SPARES)
SPLIT0 = starts([(name, 2 * n * (name in SPLIT)) for name, n in UNITS])
FIRST = ("a_qk", "up0", "b_u", "up1", "qi")
RAW_OF = [2 * UNIT0[name] + i for name, n in UNITS if name in SPLIT for i in range(2 * n)]
X_SPLIT = ["norm0", "mix_a", "norm1", "norm2", "norm3", "norm4", "mix_c"]


def signal(name, i):
    if name == "ple":
        return ("proj_done", "ple_gate")[i % 2], i // 2 + 1
    units = {"down0": 4, "down1": 4, "b_out": 2, "peer_q": 2, "att": 0.5, "conv": 0.5}.get(name, 1)
    halves = int(2 * units * (i + 1))
    if name in SPLIT:
        return "split_used", SPLIT0[name] + halves
    h = 2 * UNIT0[name] + halves - 1
    return f"raw_free{h % RING}", h // RING + 1


def bcast(ap, axis, n):
    v = ap.unsqueeze(axis)
    shape = list(v.shape)
    shape[axis] = n
    return v.to_broadcast(shape)


def build(nc, A, out):
    with ExitStack() as ctx:
        sems = {}

        def sem(name):
            if name not in sems:
                sems[name] = ctx.enter_context(nc.semaphore(name))
            return sems[name]

        def sb(name, shape, dt=F32):
            return ctx.enter_context(nc.sbuf_tensor(name, shape, dt))

        ring = sb("ring", [P, RING, HALF])
        whi = sb("whi", [P, 2, HALF], F32R)
        wlo = sb("wlo", [P, 2, HALF], F32R)
        modf = sb("mod", [P, 10 * D])
        xs = sb("xs", [P, TT, D])
        hT = sb("hT", [P, DC, TOK])
        hTh = sb("hTh", [P, DC, TOK], F32R)
        hTl = sb("hTl", [P, DC, TOK], F32R)
        ybuf = sb("ybuf", [P, TT, D])
        arena = sb("arena", [P, 12808])
        consts = sb("consts", [P, 7 * P + 16])
        ones = sb("ones", [P, P])
        wgate = sb("wgate", [P, DC, 16])
        bif = sb("bif", [P, 16])
        ncols = sb("ncols", [P, 7, DC])
        small = sb("small", [P, 1216])
        cB = sb("cB", [P, DC, P])

        ident = consts[:, 0:P]
        upper = consts[:, P:2 * P]
        causal = consts[:, 2 * P:3 * P]
        flip = consts[:, 3 * P:4 * P]
        visible = [consts[:, 4 * P:5 * P], consts[:, 5 * P:7 * P]]
        iota16 = consts[:, 7 * P:]

        def carve(buf, start, dims):
            n = 1
            for d in dims:
                n *= d
            v = buf[:, start:start + n]
            if len(dims) == 2:
                v = v.rearrange("p (a b) -> p a b", a=dims[0])
            elif len(dims) == 3:
                v = v.rearrange("p (a b c) -> p a b c", a=dims[0], b=dims[1])
            elif len(dims) == 4:
                v = v.rearrange("p (a b c d) -> p a b c d", a=dims[0], b=dims[1], c=dims[2])
            return v

        at = [0]

        def tiny(*dims):
            n = 1
            for d in dims:
                n *= d
            v = carve(small, at[0], dims)
            at[0] += n
            assert at[0] <= 1216, at[0]
            return v

        epsc = tiny(1)
        onec = tiny(1)
        ss, std, rstd = tiny(TT), tiny(TT), tiny(TT)
        mcol = tiny(2, 4, DC)
        scol = tiny(4, DC)
        ccol, csig, cact = tiny(DC), tiny(DC), tiny(DC)
        gth = tiny(TT, 16)
        gin = tiny(TT, 16)
        gii, gex, glf = tiny(TT, H), tiny(TT, H), tiny(TT, H)
        gcum = tiny(TT, 2, H)
        gr = tiny(TT, H)
        maxr, rowm, mprev, mx, nmx = tiny(TT, H), tiny(TT, H), tiny(TT, H), tiny(TT, H), tiny(TT, H)
        dif, einter, enm, mj = tiny(TT, H), tiny(TT, H), tiny(TT, H), tiny(TT, H)
        wdif, wgt = tiny(H), tiny(H)
        rsum, den, dabs, dinv = tiny(TT, H), tiny(TT, H), tiny(TT, H), tiny(TT, H)
        qnv, ssn, ssd, hroot, hfac = tiny(H), tiny(TT, H), tiny(TT, H), tiny(TT, H), tiny(TT, H)
        bst = tiny(4, 6)
        mv = tiny(TT, 2)
        lnstd, lnr = tiny(TT), tiny(TT)
        bucol = tiny(GG)
        qss, qroot, qrec = tiny(2, TT, H), tiny(2, TT, H), tiny(2, TT, H)
        qgain, kgain = tiny(AH), tiny(AH)
        wi = tiny(TT, H)
        best8 = tiny(TT, 8)
        lmax, lneg, lsum, lrec = tiny(TT, H), tiny(TT, H), tiny(TT, H), tiny(TT, H)
        cwcol, cbcol = tiny(CH // P, TAPS), tiny(CH // P)

        qT = carve(arena, 0, (4, TOK))
        kT = carve(arena, 1024, (4, TOK))
        vtok = carve(arena, 2048, (TT, H, DV))
        osig = carve(arena, 4096, (TT, D))
        dec = carve(arena, 6144, (TT, H, P))
        decT = carve(arena, 8192, (TT, H, P))
        diag = carve(arena, 8192, (TT, H, P))
        kw = carve(arena, 10240, (4 * P,))
        cbd = carve(arena, 10752, (4, 2 * DV))
        nbd = carve(arena, 11776, (4, 2))
        qc = carve(arena, 11784, (H, DV))
        hnrow = carve(arena, 10752, (D,))
        relwork = carve(arena, 11784, (RELS,))
        onehot = carve(arena, 12168, (RELS,))[0:32, :]
        relb = carve(arena, 12552, (H,))[0:32, :]
        fT = carve(arena, 0, (FF // P, TOK))
        frelu = carve(arena, 8192, (2, 4, TOK))
        uT = carve(arena, 0, (GG, TOK))
        vsg = carve(arena, 4096, (TT, GH))
        wsT = carve(arena, 8192, (GG, P))
        svb = carve(arena, 10240, (H, P))
        gain0 = carve(arena, 0, (2, D))
        gain1 = ybuf
        lng, lnb, bsrow = carve(modf, 0, (GH,)), carve(modf, 2048, (GH,)), carve(modf, 4096, (GG, P))
        bvrow = ybuf[:, :, :].rearrange("p a b -> p (a b)")
        gates = carve(modf, 0, (TT, 2 * D))
        bgrow = ybuf[:, :, :].rearrange("p a b -> p (a b)")
        relH = carve(modf, 4096, (H, TOK))
        fgrow = carve(modf, 4096, (D,))
        logit = carve(modf, 6144, (H, TOK))
        wkiwi = carve(modf, 8192, (DC, 2 * AH + H))
        qtok = carve(arena, 0, (TT, 512))
        ktok = carve(arena, 1024, (TT, 512))
        vatt = carve(arena, 2048, (TT, 512))
        qiT = carve(arena, 3072, (4, TOK))
        kiT = carve(arena, 4096, (TOK,))
        q2T = carve(arena, 4352, (4, TOK))
        k2T = carve(arena, 5376, (4, TOK))
        rel8 = carve(arena, 6400, (4, TOK))
        score = carve(arena, 7424, (TT, TOK))
        prT = carve(arena, 7936, (3, H, P))
        aT = carve(arena, 7936, (4, TOK))
        gsig = carve(arena, 2048, (4, TOK))
        qsq = carve(arena, 8960, (TT, 512))
        attT = carve(arena, 4352, (4, TOK))
        upad = carve(arena, 11008, (CH // P, TOK + TAPS - 1))
        ycT = carve(modf, 9216, (4, TOK))
        yct = carve(arena, 1024, (TT, CH))
        ysg = carve(arena, 3072, (TT, CH))
        clng = carve(arena, 12152, (CH,))
        clnb = carve(arena, 6400, (CH,))
        cT = carve(arena, 5376, (4, TOK))
        pqT = carve(arena, 0, (HC, TOK))
        skT = carve(arena, 4096, (HC, NKEYS))
        psc = carve(arena, 6144, (HC, NKEYS))
        cand = carve(arena, 8192, (H, PK, PK))
        h2 = carve(arena, 10240, (TT, D))
        gbufs = [carve(modf, 0, (4, D)), carve(arena, 0, (4, D))]
        eqc = carve(modf, 4096, (H, PK, PK))
        ptT = carve(modf, 8192, (2, TOK))
        sig = carve(arena, 6144, (TT, D))
        wproj = carve(modf, 4096, (2, D))
        sv = carve(modf, 6144, (H, 2, PK))
        sif = carve(modf, 6400, (H, 2, PK))
        topv = carve(modf, 6656, (H, PK))
        tjf = carve(modf, 6784, (2, H, PK))
        i12 = carve(modf, 7040, (2, H, PK))
        gateT = carve(modf, 7296, (TT, NSEL))
        dots = carve(modf, 7552, (TT, NSEL))
        actv = carve(modf, 7808, (TT, NSEL))
        siu = carve(modf, 8704, (H, 2, PK)).bitcast(U32)
        tju = carve(modf, 8960, (3, H, PK)).bitcast(U32)
        eidx = carve(modf, 9344, (TT, NSEL)).bitcast(U32)
        gmax, gsum, grec = tiny(H), tiny(H), tiny(H)
        icur = sb("icur", [P, GBUF], U32)

        rel_dram = nc.dram_tensor("rel_rows", (H, RELS), F32, kind="Internal").ap()

        G = ctx.enter_context(nc.psum_tensor("G", [P, 2, 2, 512], F32))
        T = ctx.enter_context(nc.psum_tensor("T", [P, 2, 512], F32))
        M = ctx.enter_context(nc.psum_tensor("M", [P, 2, 512], F32))
        M8 = M[:, :, :].rearrange("p b (j n) -> p (b j) n", n=P)
        MP = M[:, :, :].rearrange("p b (j n) -> p b j n", n=P)

        raw_full = [sem(f"raw_full{i}") for i in range(RING)]
        raw_free = [sem(f"raw_free{i}") for i in range(RING)]
        hi_done, split_used = sem("hi_done"), sem("split_used")
        g_free = [sem("g_free0"), sem("g_free1")]
        t_ready = sem("t_ready")
        t_free = [sem("t_free0"), sem("t_free1")]
        m_ready, m_free = sem("m_ready"), sem("m_free")

        block = ctx.enter_context(nc.Block())

        def block_done(eng, name, i):
            what, count = signal(name, i)
            eng.wait_ge(sem(what), count)
            return BLOCK0[name] + i

        def read_out(eng, name, i):
            b = BLOCK0[name] + i
            eng.wait_ge(g_free[b % 2], b // 2 + 1)

        def mod_part(l, m):
            at = m if l == 0 or m < 2 else 4 + m
            return modf[:, at * D:(at + 1) * D]

        def Gc(b):
            return G[:, b, :, :].rearrange("p a (c n) -> p (a c) n", n=TOK)

        def par(vals):
            return vals.rearrange("p (j b) n -> p b j n", b=2)

        @block.sync
        def _(sp):
            sp.dma_start(ccol, A["c"]).then_inc(sem("l_c"), 16)
            for h in range(RING):
                sp.dma_start(ring[:, h, :], A["wpack"][h]).then_inc(raw_full[h], 16)
                if h == 2:
                    sp.dma_start(xs[:, :, :], A["x"].rearrange("(t p) d -> p t d", p=P)).then_inc(sem("x_loaded"), 16)
            with sp.Fori(1, 2 * UNIT0["end"] // RING) as i:
                for j in range(RING):
                    sp.wait_ge(raw_free[j], i)
                    sp.dma_start(ring[:, j, :], A["wpack"][RING * i + j]).then_inc(raw_full[j], 16)
            for t in range(TT):
                sp.wait_ge(sem("out_done"), t + 1)
                sp.dma_start(out[t * P:(t + 1) * P, :], xs[:, t, :]).then_inc(sem("stored"), 16)
            sp.wait_ge(sem("stored"), 32)

        @block.gpsimd
        def _(pool):
            def load(dst, src, name):
                pool.dma_start(dst, src).then_inc(sem(name), 16)

            load(consts[:, :], A["consts"], "l_consts")
            load(onehot[:, :], A["onehot"], "l_rel")
            load(relb[:, :], A["rel_bias"], "l_rel")
            load(modf[:, 0:6 * D], A["ada_b"][0].partition_broadcast(P), "l_mod0")
            load(ncols[:, :, :], A["ncols"], "l_ncols")
            load(wgate[:, :, :], A["wgate"], "l_wgate")
            load(bif[:, :], A["b_if"].partition_broadcast(P), "l_bif")
            load(hnrow, A["hnorm_g"].partition_broadcast(P), "l_hnorm")
            for dst, name in ((qgain, "q_norm_g"), (kgain, "k_norm_g")):
                load(dst, A[name].partition_broadcast(P), "l_small")
            for dst, name in ((cwcol, "conv_w"), (cbcol, "conv_b"), (bucol, "bu")):
                load(dst, A[name], "l_small")
            pool.wait_ge(sem("columns0"), 1)
            load(modf[:, 0:2 * D], A["ada_b"][1, 0:2 * D].partition_broadcast(P), "l_mod1")
            load(modf[:, 6 * D:], A["ada_b"][1, 2 * D:].partition_broadcast(P), "l_mod1")
            pool.wait_ge(m_free, SPARE0["rel"] + 1)
            pool.dma_start(rel_dram, relwork[0:H, :]).then_inc(sem("rel_out"), 16)
            pool.wait_ge(sem("rel_out"), 16)
            pool.wait_ge(m_free, SPARE0["pv1"] + 1)
            for k in range(2):
                load(gain0[:, k, :], A["norm_g"][0, 2 * k + 1].partition_broadcast(P), "l_gain")
            pool.wait_ge(sem("x_ready"), 2)
            load(wsT, A["wsT"], "l_ws")
            load(lng, A["ln_g"].partition_broadcast(P), "l_sgu")
            load(lnb, A["ln_b"].partition_broadcast(P), "l_sgu")
            load(bsrow.rearrange("p a b -> p (a b)"), A["bs"].partition_broadcast(P), "l_sgu")
            for n in (TURN0["norm2"] + 2, TURN0["norm2"] + 3):
                pool.wait_ge(t_free[n % 2], n // 2 + 1)
            load(bvrow, A["bv"].partition_broadcast(P), "l_bv")
            for i in (2, 3):
                read_out(pool, "b_v", i)
            for k in range(2):
                load(gain1[:, k, :], A["norm_g"][1, 2 * k + 1].partition_broadcast(P), "l_gain")
            pool.wait_ge(sem("x_ready"), 4)
            load(wkiwi, A["wkiwi"], "l_kiwi")
            load(relH, bass.AP(rel_dram.tensor, 0, [[1, P], [RELS, H], [1, TOK]]), "l_relh")
            load(clng, A["conv_ln_g"].partition_broadcast(P), "l_cln")
            for n in (TURN0["norm4"] + 2, TURN0["norm4"] + 3):
                pool.wait_ge(t_free[n % 2], n // 2 + 1)
            load(bgrow[0:1, :], A["b_gate"].unsqueeze(0), "l_bgate")
            pool.wait_ge(sem("dots_done"), 3)
            load(clnb, A["conv_ln_b"].partition_broadcast(P), "l_cln")
            pool.wait_ge(m_free, SPARE0["att"])
            load(fgrow, A["ffn_norm_g"].partition_broadcast(P), "l_fg")
            for i in range(2):
                read_out(pool, "out", i)
            load(skT, A["skT"], "l_sk")
            load(ptT, A["pT"], "l_pt")
            for t in range(TT):
                pool.wait_ge(sem("eidx_ready"), t + 1)
                if t == 0:
                    pool.wait_ge(m_ready, SPARE0["psc"] + 4)
                if t == 1:
                    load(wproj, A["w_ple_proj"], "l_proj")
                for kind, table in ((0, A["peer_u"]), (1, A["peer_v"])):
                    base = (2 * t + kind) * NSEL
                    with pool.Fori(0, NSEL // GBUF) as i:
                        for j in range(GBUF):
                            pool.wait_ge(sem("row_used"), GBUF * i + (base + j + 1))
                            nc.gpsimd.tensor_copy(icur[:, j:j + 1], eidx[:, t, bass.ds(GBUF * i + j, 1)]).then_inc(sem("icur"), 1)
                            pool.wait_ge(sem("icur"), GBUF * i + (base + j + 1))
                            pool.nop(nofuse=True)
                            nc.gpsimd.indirect_dma_start(
                                out=gbufs[j // 4][:, j % 4, :], out_offset=None, in_=table,
                                in_offset=bass.IndirectOffsetOnAxis(ap=icur[:, j:j + 1], axis=0),
                            ).then_inc(sem(f"row{j}"), 16)

        @block.scalar
        def _(act):
            n_act = [0]

            def link(ins):
                n_act[0] += 1
                ins.then_inc(sem("act_step"), 1)
                act.wait_ge(sem("act_step"), n_act[0])

            made = [0]

            def split_high(q, raw, i=0):
                act.wait_ge(raw_full[raw % RING], 16 * i + 16 * (raw // RING + 1))
                if q >= 2:
                    act.wait_ge(split_used, 4 * i + (q - 1))
                nc.scalar.activation(whi[:, q % 2, :], ring[:, raw % RING, :], ACT.Copy).then_inc(hi_done, 1)

            def split_one(name, unit, half):
                q = made[0]
                assert q == SPLIT0[name] + 2 * unit + half
                split_high(q, RAW_OF[q])
                made[0] += 1

            def split(name, unit):
                for half in range(2):
                    split_one(name, unit, half)

            def x_high(name):
                for g in range(4):
                    n = TURN0[name] + g
                    act.wait_ge(t_free[n % 2], n // 2 + 1)
                    nc.scalar.activation(hTh[:, 2 * g:2 * g + 2, :], hT[:, 2 * g:2 * g + 2, :],
                                         ACT.Copy).then_inc(sem("x_high"), 1)

            def norm(n):
                if n == 0:
                    act.wait_ge(sem("x_loaded"), 16)
                    act.wait_ge(sem("consts_set"), 2)
                elif n == 5:
                    for i in range(2):
                        read_out(act, "out", i)
                else:
                    split_one(FIRST[n], 0, 0)
                    act.wait_ge(sem("x_ready"), n)
                for t in range(TT):
                    link(nc.scalar.activation(ybuf[:, t, :], xs[:, t, :], ACT.Square, accum_out=ss[:, t:t + 1]))
                nc.scalar.activation(std, ss, ACT.Sqrt, bias=epsc, scale=1.0 / D).then_inc(sem("norm_std"), 1)
                act.wait_ge(sem("norm_rstd"), n + 1)
                for t in range(TT):
                    nc.scalar.activation(ybuf[:, t, :], xs[:, t, :], ACT.Copy,
                                         scale=rstd[:, t:t + 1]).then_inc(sem("norm_xhat"), 1)
                if n == 0:
                    split_one(FIRST[n], 0, 0)
                if n < 5:
                    x_high(f"norm{n}")
                    split_one(FIRST[n], 0, 1)

            def post(name):
                if name == "b_out":
                    act.wait_ge(sem("gains"), 4)
                for nb in range(2):
                    b = block_done(act, name, nb)
                    nc.scalar.activation(ybuf[:, :, nb * 512:(nb + 1) * 512], G[:, b % 2, :, :],
                                         ACT.Copy).then_inc(g_free[b % 2], 1)
                for nb in range(2):
                    read_out(act, name, nb)
                for t in range(TT):
                    link(nc.scalar.activation(hT[:, 4 * t:4 * t + 4, :].rearrange("p a b -> p (a b)"), ybuf[:, t, :],
                                              ACT.Square, accum_out=ss[:, t:t + 1]))
                nc.scalar.activation(std, ss, ACT.Sqrt, bias=epsc, scale=1.0 / D).then_inc(sem("post_std"), 1)

            def ffn(f):
                q0, r0 = SPLIT0[f"up{f}"], 2 * UNIT0[f"up{f}"]

                def relu(u, i=0):
                    act.wait_ge(split_used, 4 * i + (q0 + 2 * u + 2))
                    act.wait_ge(sem("relu_free"), 2 * i + (8 * f + u + 1))
                    nc.scalar.activation(frelu[:, u % 2, :, :], Gc(u % 2), ACT.Relu).then_inc(g_free[u % 2], 1)

                with act.Fori(0, 3) as i:
                    for u in range(2):
                        for q in (2 * u + 2, 2 * u + 3):
                            split_high(q0 + q, r0 + q, i)
                        relu(u, i)
                made[0] += 12
                split(f"up{f}", 7)
                relu(6)
                relu(7)
                post(f"down{f}")

            act.wait_ge(sem("l_c"), 16)
            nc.scalar.activation(csig, ccol, ACT.Sigmoid).then_inc(sem("csig"), 1)
            norm(0)
            act.wait_ge(m_free, SPARE0["gates"] + 1)
            nc.scalar.activation(gth, gin, ACT.Tanh, scale=1.0 / CAP).then_inc(sem("gth"), 1)
            act.wait_ge(sem("gth"), 1)
            link(nc.scalar.activation(gex, gth[:, :, H:], ACT.Exp, scale=-CAP))
            nc.scalar.activation(glf, gex, ACT.Ln, bias=onec).then_inc(sem("glf"), 1)
            for n, (dst, scale) in enumerate(((qT, 1.0), (kT, DK ** -0.5))):
                split(("a_qk", "a_v")[n], 1 - n)
                b = block_done(act, "a_qk", n)
                nc.scalar.activation(dst, Gc(b % 2), ACT.Copy, scale=scale).then_inc(g_free[b % 2], 1)
            split("a_v", 1)
            act.wait_ge(sem("mx"), 1)
            link(nc.scalar.activation(einter, dif, ACT.Exp))
            link(nc.scalar.activation(enm, mj, ACT.Exp, scale=-1.0))
            nc.scalar.activation(wgt, wdif, ACT.Exp, scale=-1.0).then_inc(sem("wgt"), 1)
            for t in range(TT):
                for h in range(H):
                    nc.scalar.activation(dec[:, t, h, :], dec[:, t, h, :], ACT.Exp,
                                         bias=nmx[:, t, h:h + 1]).then_inc(sem("decay"), 1)
            for nb in range(2):
                b = block_done(act, "a_v", nb)
                nc.scalar.activation(vtok[:, :, 4 * nb:4 * nb + 4, :].rearrange("p t h e -> p t (h e)"),
                                     G[:, b % 2, :, :], ACT.Copy).then_inc(g_free[b % 2], 1)
                split("a_o", nb)
            for nb in range(2):
                b = block_done(act, "a_o", nb)
                nc.scalar.activation(osig[:, :, nb * 512:(nb + 1) * 512], G[:, b % 2, :, :],
                                     ACT.Sigmoid).then_inc(g_free[b % 2], 1)
            for t in range(TT):
                act.wait_ge(sem("ssd"), t + 1)
                nc.scalar.activation(hroot[:, t, :], ssd[:, t, :], ACT.Sqrt, bias=epsc).then_inc(sem("hroot"), 1)
            split_one("a_out", 0, 0)
            x_high("mix_a")
            split_one("a_out", 0, 1)
            split("a_out", 1)
            post("a_out")
            norm(1)
            ffn(0)
            norm(2)
            act.wait_ge(sem("l_small"), 80)
            for u in range(4):
                split("b_u" if u < 3 else "b_v", (u + 1) % 4)
                b = block_done(act, "b_u", u)
                for c in range(4):
                    ins = nc.scalar.activation(uT[:, 4 * u + c, :], Gc(b % 2)[:, c, :], ACT.Gelu,
                                               bias=bucol[:, 4 * u + c:4 * u + c + 1])
                ins.then_inc(g_free[b % 2], 1)
            for nb in range(4):
                if nb < 3:
                    split("b_v", nb + 1)
                read_out(act, "b_v", nb)
                v = vsg[:, :, nb * 512:(nb + 1) * 512]
                nc.scalar.activation(v, v, ACT.Gelu).then_inc(sem("v_gelu"), 1)
            for t in range(TT):
                act.wait_ge(sem("ln_var"), t + 1)
                nc.scalar.activation(lnstd[:, t:t + 1], mv[:, t, 1:2], ACT.Sqrt, bias=epsc).then_inc(sem("ln_std"), 1)
            post("b_out")
            norm(3)
            ffn(1)
            norm(4)
            split("glu", 0)
            b = block_done(act, "qi", 0)
            nc.scalar.activation(qiT, Gc(b % 2), ACT.Copy).then_inc(g_free[b % 2], 1)
            rel0 = rel8.rearrange("p a (b s) -> p (a b) s", s=P)

            def rectify(n):
                act.wait_ge(m_ready, SPARE0["dots"] + n + 1)
                if n == 0:
                    nc.scalar.activation(rel0.rearrange("p (b j) s -> p b j s", b=2), MP, ACT.Relu).then_inc(m_free, 1)
                else:
                    act.wait_ge(sem("dots_done"), n)
                    nc.scalar.activation(rel8.rearrange("p (b j) s -> p b j s", b=2),
                                         M[:, :, :].rearrange("p b (j s) -> p b j s", s=TOK),
                                         ACT.Relu).then_inc(m_free, 1)

            split("glu", 1)
            b = block_done(act, "glu", 0)
            nc.scalar.activation(aT, Gc(b % 2), ACT.Copy).then_inc(g_free[b % 2], 1)
            rectify(0)
            split("qkv", 0)
            b = block_done(act, "glu", 1)
            nc.scalar.activation(gsig, Gc(b % 2), ACT.Sigmoid).then_inc(g_free[b % 2], 1)
            rectify(1)
            for n, dst in enumerate((qtok, ktok, vatt)):
                if n < 2:
                    split("qkv", n + 1)
                else:
                    for a in range(2):
                        act.wait_ge(sem("qss"), a + 1)
                        nc.scalar.activation(qroot[:, a, :, :], qss[:, a, :, :], ACT.Sqrt, bias=epsc,
                                             scale=1.0 / AH).then_inc(sem("qroot"), 1)
                    act.wait_ge(sem("glu_done"), 1)
                b = block_done(act, "qkv", n)
                nc.scalar.activation(dst, G[:, b % 2, :, :], ACT.Copy).then_inc(g_free[b % 2], 1)
                if n == 0:
                    rectify(2)

            def gate_sigmoid(nb):
                b = block_done(act, "gates", nb)
                nc.scalar.activation(gates[:, :, nb * 512:(nb + 1) * 512], G[:, b % 2, :, :],
                                     ACT.Sigmoid).then_inc(g_free[b % 2], 1)

            def exponentials(t):
                act.wait_ge(sem("lneg"), t + 1)
                for h in range(H):
                    v = logit[:, h, 0:P * (t + 1)]
                    nc.scalar.activation(v, v, ACT.Exp, bias=lneg[:, t, h:h + 1],
                                         accum_out=lsum[:, t, h:h + 1]).then_inc(sem("probs"), 1)

            gate_sigmoid(0)
            exponentials(0)
            for nb in (1, 2):
                gate_sigmoid(nb)
            exponentials(1)
            gate_sigmoid(3)
            for t in range(TT):
                act.wait_ge(sem("cln_var"), t + 1)
                nc.scalar.activation(lnstd[:, t:t + 1], mv[:, t, 1:2], ACT.Sqrt, bias=epsc).then_inc(sem("cln_std"), 1)
            act.wait_ge(sem("cln"), 2)
            nc.scalar.activation(ysg, yct, ACT.Sigmoid).then_inc(sem("ysg"), 1)
            for u in range(2):
                split("out", u)
                if u == 0:
                    x_high("mix_c")
            norm(5)

            def queries(t, i):
                b = block_done(act, "peer_q", 2 * t + i)
                nc.scalar.activation(pqT[:, H * i:H * i + H, t * P:(t + 1) * P],
                                     G[:, b % 2, :, :].rearrange("p a (c n) -> p (a c) n", n=P),
                                     ACT.Copy).then_inc(g_free[b % 2], 1)

            def sub_scores(t, i):
                act.wait_ge(m_ready, SPARE0["psc"] + 2 * t + i + 1)
                if t:
                    act.wait_ge(sem("eidx_ready"), t)
                nc.scalar.activation(psc[:, H * i:H * i + H, :], M8, ACT.Copy).then_inc(m_free, 1)

            def gate_exp(t):
                act.wait_ge(sem("topv"), t + 1)
                nc.scalar.activation(topv, topv, ACT.Exp).then_inc(sem("gate_exp"), 1)

            def expert_gelu(t):
                act.wait_ge(sem("dots_all"), t + 1)
                nc.scalar.activation(actv[:, t, :], dots[:, t, :], ACT.Gelu_apprx_tanh).then_inc(sem("gelu"), 1)

            def embed(t):
                act.wait_ge(sem("x_ready"), 5 + t)
                link(nc.scalar.activation(ybuf[:, t, :], xs[:, t, :], ACT.Square, accum_out=ss[:, t:t + 1]))
                nc.scalar.activation(std[:, t:t + 1], ss[:, t:t + 1], ACT.Sqrt, bias=epsc,
                                     scale=1.0 / D).then_inc(sem("norm_std"), 1)
                act.wait_ge(sem("norm_rstd"), 7 + t)
                nc.scalar.activation(ybuf[:, t, :], xs[:, t, :], ACT.Copy,
                                     scale=rstd[:, t:t + 1]).then_inc(sem("norm_xhat"), 1)
                b = block_done(act, "ple", 2 * t + 1)
                nc.scalar.activation(sig[:, t, :], G[:, b % 2, :, :].rearrange("p a n -> p (a n)"),
                                     ACT.Sigmoid).then_inc(g_free[b % 2], 1)

            for i in range(2):
                queries(0, i)
                sub_scores(0, i)
            queries(1, 0)
            gate_exp(0)
            sub_scores(1, 0)
            queries(1, 1)
            sub_scores(1, 1)
            expert_gelu(0)
            gate_exp(1)
            embed(0)
            expert_gelu(1)
            embed(1)

        @block.tensor
        def _(pe):
            def raw(h):
                pe.wait_ge(raw_full[h % RING], 16 * (h // RING + 1))
                return ring[:, h % RING, :].rearrange("p (k n) -> p k n", k=DC)

            def block_free(b):
                if b >= 2:
                    pe.wait_ge(g_free[b % 2], b // 2)

            def product(dst, lhs, rhs, first=True, last=True):
                for k in range(DC):
                    ins = nc.tensor.matmul(dst, lhs(k), rhs(k), start=(first and k == 0), stop=(last and k == DC - 1))
                return ins

            def cols(b, half, w, xT, k0=0, first=True, last=True):
                for t in range(TT):
                    ins = product(G[:, b % 2, t, half * 256:(half + 1) * 256], lambda k: xT[:, k0 + k, t * P:(t + 1) * P],
                                  lambda k: w[:, k, :], first, last)
                return ins

            def rows(b, half, w, xT, first=True, last=True):
                for c in range(2):
                    ins = product(G[:, b % 2, half, c * TOK:(c + 1) * TOK], lambda k: w[:, k, c * P:(c + 1) * P],
                                  lambda k: xT[:, k, :], first, last)
                return ins

            def modulation(b, half, w, xT):
                return product(G[:, b % 2, 0, half * 256:(half + 1) * 256], lambda k: xT[:, k, :], lambda k: w[:, k, :])

            def split_half(kind, b, half, q):
                wh, wl = [buf[:, q % 2, :].rearrange("p (k n) -> p k n", k=DC) for buf in (whi, wlo)]
                for piece in range(2):
                    if kind is cols:
                        dst = G[:, b % 2, piece, half * 256:(half + 1) * 256]
                        part = slice(piece * P, (piece + 1) * P)
                        terms = [(lambda k: hTh[:, k, part], lambda k: wh[:, k, :]),
                                 (lambda k: hTl[:, k, part], lambda k: wh[:, k, :]),
                                 (lambda k: hTh[:, k, part], lambda k: wl[:, k, :])]
                    else:
                        dst = G[:, b % 2, half, piece * TOK:(piece + 1) * TOK]
                        part = slice(piece * P, (piece + 1) * P)
                        terms = [(lambda k: wh[:, k, part], lambda k: hTh[:, k, :]),
                                 (lambda k: wh[:, k, part], lambda k: hTl[:, k, :]),
                                 (lambda k: wl[:, k, part], lambda k: hTh[:, k, :])]
                    for n, (lhs, rhs) in enumerate(terms):
                        ins = product(dst, lhs, rhs, n == 0, n == 2)
                ins.then_inc(split_used, 1)

            def simple(kind, xT, name, n=None, u0=0):
                for i in range(u0, u0 + (n or dict(UNITS)[name])):
                    b = BLOCK0[name] + i
                    block_free(b)
                    for half in range(2):
                        h = 2 * (UNIT0[name] + i) + half
                        if name in SPLIT:
                            pe.wait_ge(raw_free[h % RING], h // RING + 1)
                            split_half(kind, b, half, SPLIT0[name] + 2 * i + half)
                        else:
                            kind(b, half, raw(h), xT).then_inc(raw_free[h % RING], 1)

            def x_split(name):
                pe.wait_ge(sem("x_low"), 4 * (X_SPLIT.index(name) + 1))

            def long_sum(b, xT, h0, parts):
                block_free(b)
                for half in range(2):
                    for g in range(parts):
                        h = h0 + half * parts + g
                        cols(b, half, raw(h), xT, DC * g, g == 0, g == parts - 1).then_inc(raw_free[h % RING], 1)

            def turn(name, g, pieces):
                n = TURN0[name] + g
                if n >= 2:
                    pe.wait_ge(t_free[n % 2], n // 2)
                for s, piece in enumerate(pieces):
                    ins = piece(T[:, n % 2, s * P:(s + 1) * P])
                ins.then_inc(t_ready, 1)

            def turned(name, count):
                last = TURN0[name] + count - 1
                for n in (last, last - 1):
                    if n >= 0:
                        pe.wait_ge(t_free[n % 2], n // 2 + 1)

            def flipped(src):
                return lambda dst: nc.tensor.transpose(dst[0:src.shape[1], :], src, ident)

            def turn_stream(name, src):
                for g in range(4):
                    turn(name, g, [flipped(src[:, t, c * P:(c + 1) * P]) for c in (2 * g, 2 * g + 1) for t in range(TT)])
                turned(name, 4)

            def norm(n):
                pe.wait_ge(sem("norm_xhat"), 2 * (n + 1))
                turn_stream(f"norm{n}", ybuf)

            def spare(name, i=0):
                n = SPARE0[name] + i
                if n >= 1:
                    pe.wait_ge(m_free, n)

            pe.wait_ge(sem("l_rel"), 32)
            nc.tensor.matmul(M[0:H, 0, 0:RELS], relb[:, :], onehot[:, :], start=True, stop=True).then_inc(m_ready, 1)
            pe.wait_ge(sem("cB"), 1)
            simple(modulation, cB, "ada0a")
            simple(modulation, cB, "ada0b")
            pe.wait_ge(sem("l_consts"), 16)
            norm(0)
            spare("gates")
            pe.wait_ge(sem("l_wgate"), 16)
            for t in range(TT):
                for k in range(DC):
                    ins = nc.tensor.matmul(M[:, 0, 16 * t:16 * t + 16], hT[:, k, t * P:(t + 1) * P], wgate[:, k, :],
                                           start=(k == 0), stop=(k == DC - 1))
            ins.then_inc(m_ready, 1)
            x_split("norm0")
            simple(rows, hT, "a_qk", 1)
            spare("cum")
            pe.wait_ge(sem("logf"), 1)
            for t in range(TT):
                nc.tensor.matmul(M[:, 0, 16 * t:16 * t + 8], upper, glf[:, t, :], start=True, stop=True)
                ins = nc.tensor.matmul(M[:, 0, 16 * t + 8:16 * t + 16], ones[:, :], glf[:, t, :], start=True, stop=True)
            ins.then_inc(m_ready, 1)
            simple(rows, hT, "a_qk", 1, 1)
            for t in range(TT):
                spare("rb", t)
                pe.wait_ge(sem("diag"), t + 1)
                for g in range(2):
                    ins = nc.tensor.matmul(M[:, g, :], ones[:, :],
                                           diag[:, t, 4 * g:4 * g + 4, :].rearrange("p h n -> p (h n)"),
                                           start=True, stop=True)
                ins.then_inc(m_ready, 1)
            simple(cols, hT, "a_v")
            simple(cols, hT, "a_o")
            for i in range(2):
                read_out(pe, "a_qk", i)
            turn("k_tok", 0, [flipped(kT[:, c, 0:P]) for c in range(4)])
            for t in range(TT):
                spare("score", t)
                for h in range(H):
                    r = slice(64 * (h % 2), 64 * (h % 2) + 64)
                    ins = nc.tensor.matmul(MP[:, h % 2, h // 2, :], qT[r, h // 2, t * P:(t + 1) * P],
                                           kT[r, h // 2, t * P:(t + 1) * P], start=True, stop=True)
                ins.then_inc(m_ready, 1)
                simple(modulation, cB, ("ada0c", "ada0d")[t])
            for i in range(2):
                read_out(pe, "a_v", i)
            turned("k_tok", 1)
            spare("c_loc")
            for c in range(4):
                ins = nc.tensor.matmul(M[:, c // 2, (c % 2) * 256:(c % 2) * 256 + 256], kw[:, c * P:(c + 1) * P],
                                       vtok[:, 0, 2 * c:2 * c + 2, :].rearrange("p h e -> p (h e)"),
                                       start=True, stop=True)
            ins.then_inc(m_ready, 1)
            turn("n_loc", 0, [(lambda dst, c=c: nc.tensor.matmul(dst[:, 0:1], kw[:, c * P:(c + 1) * P], ones[:, 0:1],
                                                                 start=True, stop=True)) for c in range(4)])
            for t in range(TT):
                pe.wait_ge(m_free, SPARE0["score"] + t + 1)
                for g in range(2):
                    turn("scoreT", 2 * t + g, [flipped(dec[:, t, 4 * g + s, :]) for s in range(4)])

            def pv(t):
                spare(f"pv{t}")
                for n in (TURN0["scoreT"] + 2 * t, TURN0["scoreT"] + 2 * t + 1):
                    pe.wait_ge(t_free[n % 2], n // 2 + 1)
                for h in range(H):
                    ins = nc.tensor.matmul(M8[:, h, :], decT[:, t, h, :], vtok[:, t, h, :], start=True, stop=True)
                ins.then_inc(m_ready, 1)

            simple(modulation, cB, "ada0e")
            pv(0)
            spare("qc")
            for c in range(4):
                ins = nc.tensor.matmul(M[:, c // 2, (c % 2) * 256:(c % 2) * 256 + 256], qT[:, c, P:2 * P], cbd[:, c, :],
                                       start=True, stop=True)
            ins.then_inc(m_ready, 1)
            turned("n_loc", 1)
            turn("qn", 0, [(lambda dst, c=c: nc.tensor.matmul(dst[:, 0:2], qT[:, c, P:2 * P], nbd[:, c, :],
                                                              start=True, stop=True)) for c in range(4)])
            pv(1)
            simple(modulation, cB, "ada1a")
            pe.wait_ge(sem("mixed_a"), 2)
            turn_stream("mix_a", ybuf)
            x_split("mix_a")
            simple(cols, hT, "a_out")
            simple(modulation, cB, "ada1b")

            def ffn(f):
                x_split(f"norm{2 * f + 1}")
                h0, q0, b0 = 2 * UNIT0[f"up{f}"], SPLIT0[f"up{f}"], BLOCK0[f"up{f}"]
                with pe.Fori(0, 4) as i:
                    for u in range(2):
                        pe.wait_ge(g_free[u], i + (b0 + u) // 2)
                        for half in range(2):
                            h = h0 + 2 * u + half
                            pe.wait_ge(raw_free[h % RING], i + (h // RING + 1))
                            split_half(rows, b0 + u, half, q0 + 2 * u + half)
                pe.wait_ge(sem("relu_free"), 8 * (f + 1) + 2)
                for nb in range(2):
                    long_sum(BLOCK0[f"down{f}"] + nb, fT, 2 * (UNIT0[f"down{f}"] + 4 * nb), 4)

            norm(1)
            ffn(0)
            simple(modulation, cB, "ada1c")
            norm(2)
            x_split("norm2")
            simple(rows, hT, "b_u")
            simple(cols, hT, "b_v")
            simple(modulation, cB, "ada1d")
            simple(modulation, cB, "ada1e")
            pe.wait_ge(sem("ws_masked"), 1)
            for t in range(TT):
                pe.wait_ge(sem("v_normed"), t + 1)
                for r in range(2):
                    spare("sv", 2 * t + r)
                    for j in range(8):
                        g = 8 * r + j
                        ins = nc.tensor.matmul(M8[:, j, :], vsg[:, t, g * P:(g + 1) * P], wsT[:, g, :],
                                               start=True, stop=True)
                    ins.then_inc(m_ready, 1)
            pe.wait_ge(sem("gated"), 4)
            for nb in range(2):
                long_sum(BLOCK0["b_out"] + nb, uT, 2 * (UNIT0["b_out"] + 2 * nb), 2)
            simple(modulation, cB, "ada1f")
            norm(3)
            ffn(1)
            norm(4)
            spare("kiwi")
            pe.wait_ge(sem("l_kiwi"), 16)
            for k in range(DC):
                nc.tensor.matmul(M[:, 0, 0:TOK], wkiwi[:, k, 0:2 * AH], hT[:, k, :], start=(k == 0), stop=(k == DC - 1))
            for t in range(TT):
                for k in range(DC):
                    ins = nc.tensor.matmul(M[:, 1, H * t:H * t + H], hT[:, k, t * P:(t + 1) * P],
                                           wkiwi[:, k, 2 * AH:], start=(k == 0), stop=(k == DC - 1))
            ins.then_inc(m_ready, 1)
            x_split("norm4")
            simple(rows, hT, "qi")
            for i, (t, h0, nh) in enumerate(((0, 0, 8), (1, 0, 4), (1, 4, 4))):
                simple(*((rows, hT, "glu", 1, 0), (rows, hT, "glu", 1, 1), (cols, hT, "qkv", 1, 0))[i])
                if i == 0:
                    pe.wait_ge(m_free, SPARE0["kiwi"] + 1)
                    read_out(pe, "qi", 0)
                spare("dots", i)
                keys = P * (t + 1)
                for h in range(h0, h0 + nh):
                    r = slice(64 * (h % 2), 64 * (h % 2) + 64)
                    s = (h - h0) // 2
                    ins = nc.tensor.matmul(M[:, h % 2, s * keys:(s + 1) * keys], qiT[r, h // 2, t * P:(t + 1) * P],
                                           kiT[r, 0:keys], start=True, stop=True)
                ins.then_inc(m_ready, 1)
            simple(cols, hT, "qkv", 2, 1)
            pe.wait_ge(sem("l_bgate"), 16)

            def gate_product(nb):
                b = BLOCK0["gates"] + nb
                block_free(b)
                for half in range(2):
                    h, c0 = 2 * (UNIT0["gates"] + nb) + half, 512 * nb + 256 * half
                    w = raw(h)
                    for t in range(TT):
                        dst = G[:, b % 2, t, 256 * half:256 * (half + 1)]
                        nc.tensor.matmul(dst, ones[0:1, :], bgrow[0:1, c0:c0 + 256], start=True, stop=False)
                        ins = product(dst, lambda k: hT[:, k, t * P:(t + 1) * P], lambda k: w[:, k, :], False)
                    ins.then_inc(raw_free[h % RING], 1)

            gate_product(0)
            for a, (name, src) in enumerate((("qT", qtok), ("kT", ktok))):
                pe.wait_ge(sem("qk_normed"), a + 1)
                for g in range(2):
                    turn(name, g, [flipped(src[:, t, c * P:(c + 1) * P]) for c in (2 * g, 2 * g + 1) for t in range(TT)])
            gate_product(1)
            turned("qT", 2)
            turned("kT", 2)
            pe.wait_ge(sem("l_relh"), 16)

            def logits(i, t, h0, nh):
                spare("logit", i)
                keys = P * (t + 1)
                for h in range(h0, h0 + nh):
                    r = slice(64 * (h % 2), 64 * (h % 2) + 64)
                    s = (h - h0) // 2
                    dst = M[:, h % 2, s * keys:(s + 1) * keys]
                    nc.tensor.matmul(dst, q2T[r, h // 2, t * P:(t + 1) * P], k2T[r, h // 2, 0:keys],
                                     start=True, stop=False)
                    ins = nc.tensor.matmul(dst, flip, relH[:, h, P - P * t:P - P * t + keys], start=False, stop=True)
                ins.then_inc(m_ready, 1)

            def probs(t, kt):
                pe.wait_ge(sem("probs_normed"), t + 1)
                for g in range(2):
                    turn("probT", 2 * (t + kt) + g,
                         [flipped(logit[:, 4 * g + s, kt * P:(kt + 1) * P]) for s in range(4)])

            logits(0, 0, 0, 8)
            gate_product(2)
            probs(0, 0)
            logits(1, 1, 0, 4)
            logits(2, 1, 4, 4)
            gate_product(3)
            probs(1, 0)
            probs(1, 1)
            turned("probT", 6)
            read_out(pe, "qkv", 2)
            spare("att")
            for t in range(TT):
                for h in range(H):
                    r = slice(64 * (h % 2), 64 * (h % 2) + 64)
                    for kt in range(t + 1):
                        ins = nc.tensor.matmul(M[r, t, (h // 2) * P:(h // 2 + 1) * P], vatt[:, kt, h * AH:(h + 1) * AH],
                                               prT[:, t + kt, h, :], start=(kt == 0), stop=(kt == t))
            ins.then_inc(m_ready, 1)
            pe.wait_ge(sem("tap"), CH // P * TAPS)
            for g in range(2):
                turn("conv_tok", g, [flipped(ycT[:, 2 * g + s // 2, (s % 2) * P:(s % 2 + 1) * P]) for s in range(4)])
            pe.wait_ge(m_free, SPARE0["att"] + 1)
            for name, xT in (("att", attT), ("conv", cT)):
                if name == "conv":
                    pe.wait_ge(sem("silu"), 1)
                    for g in range(2):
                        turn("convT", g, [flipped(yct[:, t, c * P:(c + 1) * P]) for c in (2 * g, 2 * g + 1) for t in range(TT)])
                    turned("convT", 2)
                for nb in range(2):
                    h, b = 2 * UNIT0[name] + nb, BLOCK0[name] + nb
                    raw(h)
                    w = ring[:, h % RING, :].rearrange("p (k n) -> p k n", k=4)
                    block_free(b)
                    for t in range(TT):
                        for k in range(4):
                            ins = nc.tensor.matmul(G[:, b % 2, t, :], xT[:, k, t * P:(t + 1) * P], w[:, k, :],
                                                   start=(k == 0), stop=(k == 3))
                    ins.then_inc(raw_free[h % RING], 1)
            pe.wait_ge(sem("mixed_c"), 2)
            turn_stream("mix_c", ybuf)
            x_split("mix_c")
            simple(cols, hT, "out")
            norm(5)
            for t in range(TT):
                for i in range(2):
                    b = BLOCK0["peer_q"] + 2 * t + i
                    block_free(b)
                    for u in range(2):
                        for half in range(2):
                            h = 2 * (UNIT0["peer_q"] + 4 * t + 2 * i + u) + half
                            w = raw(h)
                            for c in range(2):
                                ins = product(G[:, b % 2, u, (2 * half + c) * P:(2 * half + c + 1) * P],
                                              lambda k: w[:, k, c * P:(c + 1) * P], lambda k: hT[:, k, t * P:(t + 1) * P])
                            ins.then_inc(raw_free[h % RING], 1)
                    if (t, i) == (0, 0):
                        pe.wait_ge(sem("l_sk"), 16)
                    read_out(pe, "peer_q", 2 * t + i)
                    spare("psc", 2 * t + i)
                    for j in range(H):
                        ins = nc.tensor.matmul(M8[:, j, :], pqT[:, H * i + j, t * P:(t + 1) * P], skT[:, H * i + j, :],
                                               start=True, stop=True)
                    ins.then_inc(m_ready, 1)
            pe.wait_ge(sem("l_pt"), 16)
            pe.wait_ge(sem("l_proj"), 16)
            for t in range(TT):
                b = BLOCK0["ple"] + 2 * t
                block_free(b)
                for nb in range(2):
                    for k in range(2):
                        ins = nc.tensor.matmul(G[:, b % 2, nb, :], ptT[:, k, t * P:(t + 1) * P],
                                               wproj[:, k, nb * 512:(nb + 1) * 512], start=(k == 0), stop=(k == 1))
                ins.then_inc(sem("proj_done"), 1)
                pe.wait_ge(sem("norm_xhat"), 13 + t)
                for g in range(2):
                    turn("norm6", 2 * t + g, [flipped(ybuf[:, t, c * P:(c + 1) * P]) for c in range(4 * g, 4 * g + 4)])
                turned("norm6", 2 * t + 2)
                b += 1
                block_free(b)
                for h in range(4):
                    w = raw(2 * UNIT0["ple"] + h)
                    ins = product(G[:, b % 2, h // 2, h % 2 * 256:(h % 2 + 1) * 256],
                                  lambda k: hT[:, k, t * P:(t + 1) * P], lambda k: w[:, k, :])
                ins.then_inc(sem("ple_gate"), 1)

        @block.vector
        def _(dve):
            V = nc.vector
            n_dve = [0]

            def link(ins):
                n_dve[0] += 1
                ins.then_inc(sem("dve_step"), 1)
                dve.wait_ge(sem("dve_step"), n_dve[0])

            def turn_done(name, g):
                n = TURN0[name] + g
                dve.wait_ge(t_ready, n + 1)
                return n % 2

            def spare_done(name, i=0):
                dve.wait_ge(m_ready, SPARE0[name] + i + 1)

            def spare_read(ins, name, i=0):
                ins.then_inc(m_free, 1)
                dve.wait_ge(m_free, SPARE0[name] + i + 1)

            def block_read(ins, name, i):
                ins.then_inc(g_free[(BLOCK0[name] + i) % 2], 1)

            def copies(name, groups):
                for g, dst in enumerate(groups):
                    p = turn_done(name, g)
                    V.tensor_copy(dst, T[:, p, :]).then_inc(t_free[p], 1)

            made = [0]

            def split_low(q, raw, i=0):
                dve.wait_ge(hi_done, 4 * i + (q + 1))
                V.tensor_tensor(wlo[:, q % 2, :], ring[:, raw % RING, :], whi[:, q % 2, :].bitcast(F32),
                                ALU.subtract).then_inc(raw_free[raw % RING], 1)

            def split_one(name, unit, half):
                q = made[0]
                assert q == SPLIT0[name] + 2 * unit + half
                split_low(q, RAW_OF[q])
                made[0] += 1

            def split(name, unit):
                for half in range(2):
                    split_one(name, unit, half)

            def x_parts(name, evac):
                for g in range(5):
                    if g < 4:
                        evac(g)
                    if g > 0:
                        c = slice(2 * g - 2, 2 * g)
                        dve.wait_ge(sem("x_high"), 4 * X_SPLIT.index(name) + g)
                        V.tensor_tensor(hTl[:, c, :], hT[:, c, :], hTh[:, c, :].bitcast(F32),
                                        ALU.subtract).then_inc(sem("x_low"), 1)

            def turned_in(name):
                def evac(g):
                    p = turn_done(name, g)
                    V.tensor_copy(hT[:, 2 * g:2 * g + 2, :].rearrange("p c n -> p (c n)"), T[:, p, :]).then_inc(t_free[p], 1)
                x_parts(name, evac)

            def modulations(name):
                l, first = ADA[name]
                dve.wait_ge(sem(f"l_mod{l}"), 16 + 16 * l)
                for i in range(dict(UNITS)[name]):
                    b = block_done(dve, name, i)
                    m, k = (first + i) // 2, (first + i) % 2
                    part = mod_part(l, m)[:, k * 512:(k + 1) * 512]
                    block_read(V.tensor_tensor(part, part, G[:, b % 2, 0, :], ALU.add), name, i)
                for i in range(dict(UNITS)[name]):
                    read_out(dve, name, i)

            def column(l, m, k):
                work = carve(arena, 8192 if (l, k) < (0, 2) else 10240, (DC, P))
                link(V.tensor_tensor(work, mod_part(l, m).rearrange("p (c n) -> p c n", n=P),
                                     bcast(ident, 1, DC), ALU.mult))
                link(V.tensor_reduce(mcol[:, l, k, :], work, AX_X, ALU.add))

            def scale_column(l, half):
                link(V.scalar_tensor_tensor(out=scol[:, 2 * l + half, :], in0=mcol[:, l, 2 * half + 1, :], scalar=1.0,
                                            in1=ncols[:, 2 * l + half, :], op0=ALU.add, op1=ALU.mult))

            def gain_row(l, half):
                dve.wait_ge(sem("l_gain"), 32 * (l + 1))
                part = mod_part(l, 3 * half + 2)
                V.tensor_tensor(part, part, (gain0, gain1)[l][:, half, :], ALU.mult).then_inc(sem("gains"), 1)
                dve.wait_ge(sem("gains"), 2 * l + half + 1)

            def norm(n, filler=None):
                dve.wait_ge(sem("norm_std"), n + 1)
                V.reciprocal(rstd, std).then_inc(sem("norm_rstd"), 1)
                if filler:
                    modulations(filler)
                if n == 3:
                    column(1, 3, 2)
                if 0 < n < 5:
                    split_one(FIRST[n], 0, 0)

                def evac(g):
                    p = turn_done(f"norm{n}", g)
                    for c in (2 * g, 2 * g + 1):
                        src = T[:, p, (c % 2) * TOK:(c % 2 + 1) * TOK]
                        if n < 4:
                            ins = V.tensor_scalar(hT[:, c, :], src, scol[:, n, c:c + 1],
                                                  mcol[:, n // 2, 2 * (n % 2), c:c + 1], ALU.mult, ALU.add)
                        else:
                            ins = V.tensor_scalar(hT[:, c, :], src, ncols[:, n, c:c + 1], None, ALU.mult)
                    ins.then_inc(t_free[p], 1)

                if n < 5:
                    x_parts(f"norm{n}", evac)
                    if n == 0:
                        split_one(FIRST[n], 0, 0)
                    split_one(FIRST[n], 0, 1)
                else:
                    for g in range(4):
                        evac(g)

            def post(p):
                l, half = p // 2, p % 2
                dve.wait_ge(sem("post_std"), p + 1)
                link(V.reciprocal(rstd, std))
                row = mod_part(l, 3 * half + 2)
                for t in range(TT):
                    link(V.scalar_tensor_tensor(out=ybuf[:, t, :], in0=ybuf[:, t, :], scalar=rstd[:, t:t + 1], in1=row,
                                                op0=ALU.mult, op1=ALU.mult))
                    ins = V.tensor_tensor(xs[:, t, :], xs[:, t, :], ybuf[:, t, :], ALU.add)
                    if t == 0:
                        link(ins)
                ins.then_inc(sem("x_ready"), 1)

            def squares(f):
                q0, r0, b0 = SPLIT0[f"up{f}"], 2 * UNIT0[f"up{f}"], BLOCK0[f"up{f}"]

                def square(u, i=0):
                    dve.wait_ge(g_free[u % 2], i + ((b0 + u) // 2 + 1))
                    r = frelu[:, u % 2, :, :]
                    V.tensor_tensor(fT[:, bass.ds(8 * i + 4 * u, 4), :], r, r, ALU.mult).then_inc(sem("relu_free"), 1)

                with dve.Fori(0, 3) as i:
                    for u in range(2):
                        for q in (2 * u + 2, 2 * u + 3):
                            split_low(q0 + q, r0 + q, i)
                        square(u, i)
                made[0] += 12
                split(f"up{f}", 7)
                square(6)
                square(7)

            V.memset(epsc, EPS).then_inc(sem("consts_set"), 1)
            V.memset(onec, 1.0).then_inc(sem("consts_set"), 1)
            V.memset(ones[:, :], 1.0).then_inc(sem("ones_set"), 1)
            for name, n in (("relu_free", 2), ("row_used", GBUF)):
                for k in range(n):
                    V.memset(mprev[:, 0, :], 0.0).then_inc(sem(name), 1)
                    dve.wait_ge(sem(name), k + 1)
            dve.wait_ge(sem("csig"), 1)
            link(V.tensor_tensor(cact, ccol, csig, ALU.mult))
            V.tensor_copy(cB[:, :, :], bcast(cact, 2, P)).then_inc(sem("cB"), 1)
            spare_done("rel")
            spare_read(V.tensor_copy(relwork[0:H, :], M[0:H, 0, 0:RELS]), "rel")
            modulations("ada0a")
            dve.wait_ge(sem("l_consts"), 16)
            dve.wait_ge(sem("l_ncols"), 16)
            column(0, 0, 0)
            column(0, 1, 1)
            V.scalar_tensor_tensor(out=scol[:, 0, :], in0=mcol[:, 0, 1, :], scalar=1.0, in1=ncols[:, 0, :],
                                   op0=ALU.add, op1=ALU.mult).then_inc(sem("columns0"), 1)
            dve.wait_ge(sem("columns0"), 1)
            norm(0, "ada0b")
            dve.wait_ge(sem("l_bif"), 16)
            spare_done("gates")
            spare_read(V.tensor_tensor(gin, M[:, 0, 0:32].rearrange("p (t n) -> p t n", t=TT), bcast(bif[:, :], 1, TT),
                                       ALU.add), "gates")
            dve.wait_ge(sem("gth"), 1)
            link(V.tensor_scalar(gii, gth[:, :, 0:H], CAP, None, ALU.mult))
            dve.wait_ge(sem("glf"), 1)
            V.tensor_scalar(glf, glf, -1.0, None, ALU.mult).then_inc(sem("logf"), 1)
            split("a_qk", 1)
            spare_done("cum")
            spare_read(V.tensor_copy(gcum, M[:, 0, 0:32].rearrange("p (t a n) -> p t a n", t=TT, a=2)), "cum")
            link(V.tensor_tensor(gr, gii, gcum[:, :, 0, :], ALU.subtract))
            for t in range(TT):
                V.tensor_tensor(diag[:, t, :, :], bcast(ident, 1, H), bcast(gr[:, t, :], 2, P), ALU.mult).then_inc(sem("diag"), 1)
            split("a_v", 0)
            for t in range(TT):
                spare_done("rb", t)
                link(V.tensor_reduce(maxr[:, t, :], M8, AX_X, ALU.max))
                spare_read(V.tensor_tensor(dec[:, t, :, :], M8, bcast(causal, 1, H), ALU.add), "rb", t)
                link(V.tensor_reduce(rowm[:, t, :], dec[:, t, :, :], AX_X, ALU.max))
            split("a_v", 1)
            link(V.scalar_tensor_tensor(out=mprev[:, 1, :], in0=maxr[:, 0, :], scalar=0.0, in1=gcum[:, 0, 1, :],
                                        op0=ALU.max, op1=ALU.add))
            link(V.tensor_tensor(mx, mprev, rowm, ALU.max))
            link(V.tensor_scalar(nmx, mx, -1.0, None, ALU.mult))
            link(V.tensor_tensor(dif, mprev, mx, ALU.subtract))
            link(V.tensor_tensor(mj, gcum[:, :, 0, :], mx, ALU.add))
            V.scalar_tensor_tensor(out=wdif, in0=maxr[:, 0, :], scalar=0.0, in1=gr[:, 0, :],
                                   op0=ALU.max, op1=ALU.subtract).then_inc(sem("mx"), 1)
            for i in range(2):
                split("a_o", i)
            for i in range(2):
                read_out(dve, "a_o", i)
            dve.wait_ge(sem("l_hnorm"), 16)
            for t in range(TT):
                link(V.tensor_tensor(osig[:, t, :], osig[:, t, :], hnrow, ALU.mult))
            link(V.memset(cbd, 0.0))
            link(V.memset(nbd, 0.0))
            dve.wait_ge(sem("wgt"), 1)
            p = turn_done("k_tok", 0)
            V.tensor_tensor(kw.rearrange("p (h d) -> p h d", h=H), T[:, p, :].rearrange("p (h d) -> p h d", h=H),
                            bcast(wgt, 2, DK), ALU.mult).then_inc(t_free[p], 1)
            for t in range(TT):
                spare_done("score", t)
                dve.wait_ge(sem("decay"), H * (t + 1))
                d = par(dec[:, t, :, :])
                spare_read(V.tensor_tensor(d, MP, d, ALU.mult), "score", t)
                link(V.tensor_reduce(rsum[:, t, :], dec[:, t, :, :], AX_X, ALU.add))
                modulations(("ada0c", "ada0d")[t])
            spare_done("c_loc")
            m4 = M[:, :, :].rearrange("p b (c n) -> p (b c) n", n=2 * DV)
            link(V.tensor_copy(cbd[0:DK, :, 0:DV], m4[0:DK, :, 0:DV]))
            spare_read(V.tensor_copy(cbd[DK:P, :, DV:], m4[DK:P, :, DV:]), "c_loc")
            p = turn_done("n_loc", 0)
            t4 = T[:, p, :].rearrange("p (c n) -> p c n", c=4)
            link(V.tensor_copy(nbd[0:DK, :, 0:1], t4[0:DK, :, 0:1]))
            V.tensor_copy(nbd[DK:P, :, 1:2], t4[DK:P, :, 0:1]).then_inc(t_free[p], 1)
            copies("scoreT", [decT[:, t, 4 * g:4 * g + 4, :].rearrange("p h n -> p (h n)") for t in range(TT) for g in range(2)])
            modulations("ada0e")
            spare_done("pv0")
            spare_read(V.tensor_copy(dec[:, 0, :, :], M8), "pv0")
            dve.wait_ge(sem("rel_out"), 16)
            spare_done("qc")
            spare_read(V.tensor_tensor(qc, M8, bcast(einter[:, 1, :], 2, DV), ALU.mult), "qc")
            p = turn_done("qn", 0)
            V.tensor_copy(qnv.rearrange("p (c n) -> p c n", c=4),
                          T[:, p, :].rearrange("p (c n) -> p c n", c=4)[:, :, 0:2]).then_inc(t_free[p], 1)
            dve.wait_ge(t_free[p], (TURN0["qn"] // 2) + 1)
            spare_done("pv1")
            spare_read(V.tensor_tensor(dec[:, 1, :, :], M8, qc, ALU.add), "pv1")
            link(V.tensor_copy(den[:, 0, :], rsum[:, 0, :]))
            link(V.tensor_tensor(den[:, 1, :], qnv, einter[:, 1, :], ALU.mult))
            link(V.tensor_tensor(den[:, 1, :], den[:, 1, :], rsum[:, 1, :], ALU.add))
            link(V.scalar_tensor_tensor(out=dabs, in0=den, scalar=-1.0, in1=den, op0=ALU.mult, op1=ALU.max))
            link(V.tensor_tensor(dabs, dabs, enm, ALU.max))
            link(V.reciprocal(dinv, dabs))
            link(V.tensor_tensor(dabs, dinv, dinv, ALU.mult))
            for t in range(TT):
                link(V.tensor_tensor(decT[:, t, :, :], dec[:, t, :, :], dec[:, t, :, :], ALU.mult))
                link(V.tensor_reduce(ssn[:, t, :], decT[:, t, :, :], AX_X, ALU.add))
                V.scalar_tensor_tensor(out=ssd[:, t, :], in0=ssn[:, t, :], scalar=1.0 / DV, in1=dabs[:, t, :],
                                       op0=ALU.mult, op1=ALU.mult).then_inc(sem("ssd"), 1)
            for t in range(TT):
                dve.wait_ge(sem("hroot"), t + 1)
                link(V.reciprocal(hfac[:, t, :], hroot[:, t, :]))
                link(V.tensor_tensor(hfac[:, t, :], hfac[:, t, :], dinv[:, t, :], ALU.mult))
                link(V.tensor_tensor(dec[:, t, :, :], dec[:, t, :, :], bcast(hfac[:, t, :], 2, DV), ALU.mult))
                V.tensor_tensor(ybuf[:, t, :], dec[:, t, :, :].rearrange("p h n -> p (h n)"), osig[:, t, :],
                                ALU.mult).then_inc(sem("mixed_a"), 1)
            modulations("ada1a")
            split_one("a_out", 0, 0)
            turned_in("mix_a")
            split_one("a_out", 0, 1)
            split("a_out", 1)
            column(0, 3, 2)
            column(0, 4, 3)
            scale_column(0, 1)
            gain_row(0, 0)
            gain_row(0, 1)
            post(0)
            norm(1, "ada1b")
            squares(0)
            column(1, 0, 0)
            column(1, 1, 1)
            scale_column(1, 0)
            post(1)
            norm(2, "ada1c")
            dve.wait_ge(sem("l_ws"), 16)
            V.tensor_tensor(wsT, wsT, bcast(upper, 1, GG), ALU.mult).then_inc(sem("ws_masked"), 1)
            for u in (1, 2, 3):
                split("b_u", u)
            split("b_v", 0)
            dve.wait_ge(sem("l_bv"), 16)
            for nb in range(4):
                if nb < 3:
                    split("b_v", nb + 1)
                b = block_done(dve, "b_v", nb)
                block_read(V.tensor_tensor(vsg[:, :, nb * 512:(nb + 1) * 512], G[:, b % 2, :, :],
                                           bcast(bvrow[:, nb * 512:(nb + 1) * 512], 1, TT), ALU.add), "b_v", nb)
            dve.wait_ge(sem("v_gelu"), 4)
            dve.wait_ge(sem("l_sgu"), 48)
            for t in range(TT):
                for q in range(4):
                    link(V.bn_stats(bst[:, q, :], vsg[:, t, q * 512:(q + 1) * 512]))
                V.bn_aggr(mv[:, t, :], bst).then_inc(sem("ln_var"), 1)
                dve.wait_ge(sem("ln_std"), t + 1)
                link(V.reciprocal(lnr[:, t:t + 1], lnstd[:, t:t + 1]))
                v = vsg[:, t, :]
                link(V.tensor_scalar(v, v, mv[:, t, 0:1], lnr[:, t:t + 1], ALU.subtract, ALU.mult))
                link(V.tensor_tensor(v, v, lng, ALU.mult))
                V.tensor_tensor(v, v, lnb, ALU.add).then_inc(sem("v_normed"), 1)
                modulations(("ada1d", "ada1e")[t])
            for i in range(4):
                read_out(dve, "b_u", i)
            for t in range(TT):
                for r in range(2):
                    spare_done("sv", 2 * t + r)
                    spare_read(V.tensor_tensor(svb, M8, bsrow[:, 8 * r:8 * r + 8, :], ALU.add), "sv", 2 * t + r)
                    u = uT[:, 8 * r:8 * r + 8, t * P:(t + 1) * P]
                    V.tensor_tensor(u, u, svb, ALU.mult).then_inc(sem("gated"), 1)
                    dve.wait_ge(sem("gated"), 2 * t + r + 1)
            column(1, 4, 3)
            scale_column(1, 1)
            gain_row(1, 0)
            gain_row(1, 1)
            post(2)
            norm(3, "ada1f")
            squares(1)
            post(3)
            norm(4)
            spare_done("kiwi")
            link(V.tensor_copy(kiT, M[:, 0, 0:TOK]))
            spare_read(V.tensor_copy(wi, M[:, 1, 0:2 * H].rearrange("p (t h) -> p t h", t=TT)), "kiwi")
            rel0 = rel8.rearrange("p a (b s) -> p (a b) s", s=P)

            def add_head(t, h, dot):
                sc = score[:, t, 0:P * (t + 1)]
                if h == 0:
                    return V.tensor_scalar(sc, dot, wi[:, t, h:h + 1], None, ALU.mult)
                return V.scalar_tensor_tensor(out=sc, in0=dot, scalar=wi[:, t, h:h + 1], in1=sc, op0=ALU.mult, op1=ALU.add)

            def conv(c0, w0, w1):
                for w in range(w0, w1):
                    for c in (c0, c0 + 1):
                        src = upad[:, c, w:w + TOK]
                        if w == 0:
                            ins = V.tensor_scalar(ycT[:, c, :], src, cwcol[:, c, 0:1], cbcol[:, c:c + 1], ALU.mult, ALU.add)
                        else:
                            dve.wait_ge(sem("tap"), (c0 // 2) * 2 * TAPS + 2 * w + c - c0 - 1)
                            ins = V.scalar_tensor_tensor(out=ycT[:, c, :], in0=src, scalar=cwcol[:, c, w:w + 1],
                                                         in1=ycT[:, c, :], op0=ALU.mult, op1=ALU.add)
                        ins.then_inc(sem("tap"), 1)

            split("glu", 0)
            for i, (t, h0, nh) in enumerate(((0, 0, 8), (1, 0, 4), (1, 4, 4))):
                split(*(("glu", 1), ("qkv", 0), ("qkv", 1))[i])
                dve.wait_ge(m_free, SPARE0["dots"] + i + 1)
                for h in range(nh):
                    src = rel0 if t == 0 else rel8
                    ins = add_head(t, h0 + h, src[:, (h % 2) * (nh // 2) + h // 2, :])
                    if h < nh - 1:
                        link(ins)
                ins.then_inc(sem("dots_done"), 1)
                dve.wait_ge(sem("dots_done"), i + 1)
                if i == 1:
                    for nb in range(2):
                        read_out(dve, "glu", nb)
                    link(V.memset(upad[:, :, 0:TAPS - 1], 0.0))
                    V.tensor_tensor(upad[:, :, TAPS - 1:], aT, gsig, ALU.mult).then_inc(sem("glu_done"), 1)
                    dve.wait_ge(sem("glu_done"), 1)
            conv(0, 0, 6)
            split("qkv", 2)
            for a, (src, gain) in enumerate(((qtok, qgain), (ktok, kgain))):
                read_out(dve, "qkv", a)
                if a == 1:
                    conv(0, 6, 12)
                link(V.tensor_tensor(qsq, src, src, ALU.mult))
                V.tensor_reduce(qss[:, a, :, :], qsq.rearrange("p t (h d) -> p t h d", h=H), AX_X, ALU.add).then_inc(sem("qss"), 1)
                dve.wait_ge(sem("qss"), a + 1)
            dve.wait_ge(sem("l_small"), 80)
            for a, (src, gain) in enumerate(((qtok, qgain), (ktok, kgain))):
                dve.wait_ge(sem("qroot"), a + 1)
                link(V.reciprocal(qrec[:, a, :, :], qroot[:, a, :, :]))
                if a == 0:
                    link(V.tensor_scalar(qrec[:, a, :, :], qrec[:, a, :, :], AH ** -0.5, None, ALU.mult))
                v = src.rearrange("p t (h d) -> p (t h) d", h=H)
                link(V.tensor_tensor(v, v, bcast(qrec[:, a, :, :].rearrange("p t h -> p (t h)"), 2, AH), ALU.mult))
                V.tensor_tensor(v, v, bcast(gain, 1, TT * H), ALU.mult).then_inc(sem("qk_normed"), 1)
            seen = [score[:, t, 0:P * (t + 1)] for t in range(TT)]

            def each_tile(op):
                for t in range(TT):
                    dve.wait_ge(sem("dve_step"), n_dve[0] - 1)
                    op(t, seen[t]).then_inc(sem("dve_step"), 1)
                    n_dve[0] += 1

            each_tile(lambda t, sc: V.scalar_tensor_tensor(out=sc, in0=sc, scalar=AH ** -0.5 * H ** -0.5,
                                                           in1=visible[t], op0=ALU.mult, op1=ALU.add))
            for _ in range(TOPK // 8):
                each_tile(lambda t, sc: V.max(best8[:, t, :], sc))
                each_tile(lambda t, sc: V.match_replace(sc, best8[:, t, :], sc, TAKEN))
            each_tile(lambda t, sc: V.tensor_scalar(sc, sc, TAKEN / 2, NEG, ALU.is_gt, ALU.mult))
            dve.wait_ge(sem("dve_step"), n_dve[0])
            copies("qT", [q2T[:, 2 * g:2 * g + 2, :].rearrange("p c n -> p (c n)") for g in range(2)])
            copies("kT", [k2T[:, 2 * g:2 * g + 2, :].rearrange("p c n -> p (c n)") for g in range(2)])
            def softmax(t):
                v = logit[:, :, 0:P * (t + 1)]
                link(V.tensor_reduce(lmax[:, t, :], v, AX_X, ALU.max))
                V.tensor_scalar(lneg[:, t, :], lmax[:, t, :], -1.0, None, ALU.mult).then_inc(sem("lneg"), 1)

            def probabilities(t):
                v = logit[:, :, 0:P * (t + 1)]
                dve.wait_ge(sem("probs"), H * (t + 1))
                link(V.reciprocal(lrec[:, t, :], lsum[:, t, :]))
                V.tensor_tensor(v, v, bcast(lrec[:, t, :], 2, P * (t + 1)), ALU.mult).then_inc(sem("probs_normed"), 1)
                for g in range(2 * t, 4 * t + 2):
                    p = turn_done("probT", g)
                    V.tensor_copy(prT[:, g // 2, 4 * (g % 2):4 * (g % 2) + 4, :].rearrange("p h n -> p (h n)"),
                                  T[:, p, :]).then_inc(t_free[p], 1)

            conv(0, 12, 28)
            spare_done("logit")
            spare_read(V.tensor_tensor(par(logit[:, :, 0:P]), MP, bcast(bcast(score[:, 0, 0:P], 1, 4), 1, 2), ALU.add), "logit")
            softmax(0)
            conv(0, 28, TAPS)
            conv(2, 0, 3)
            probabilities(0)
            for r in range(2):
                spare_done("logit", 1 + r)
                spare_read(V.tensor_tensor(par(logit[:, 4 * r:4 * r + 4, :]), M[:, :, :].rearrange("p b (j n) -> p b j n", n=TOK),
                                           bcast(bcast(score[:, 1, :], 1, 2), 1, 2), ALU.add), "logit", 1 + r)
            softmax(1)
            conv(2, 3, 14)
            probabilities(1)
            conv(2, 14, TAPS)
            spare_done("att")
            spare_read(V.tensor_copy(attT.rearrange("p c (t n) -> p t c n", t=TT), MP), "att")
            for g in range(2):
                p = turn_done("conv_tok", g)
                V.tensor_copy(yct[:, :, 2 * g * P:(2 * g + 2) * P].rearrange("p t (c n) -> p t c n", c=2),
                              T[:, p, :].rearrange("p (c t n) -> p t c n", c=2, t=TT)).then_inc(t_free[p], 1)
            for g in range(2):
                n = TURN0["conv_tok"] + g
                dve.wait_ge(t_free[n % 2], n // 2 + 1)
            dve.wait_ge(sem("l_cln"), 32)
            for t in range(TT):
                v = yct[:, t, :]
                link(V.bn_stats(bst[:, 0, :], v))
                V.bn_aggr(mv[:, t, :], bst[:, 0:1, :]).then_inc(sem("cln_var"), 1)
                dve.wait_ge(sem("cln_std"), t + 1)
                link(V.reciprocal(lnr[:, t:t + 1], lnstd[:, t:t + 1]))
                link(V.tensor_scalar(v, v, mv[:, t, 0:1], lnr[:, t:t + 1], ALU.subtract, ALU.mult))
                link(V.tensor_tensor(v, v, clng, ALU.mult))
                V.tensor_tensor(v, v, clnb, ALU.add).then_inc(sem("cln"), 1)
            for nb in (2, 3):
                read_out(dve, "gates", nb)
            for nb in range(2):
                b = block_done(dve, "att", nb)
                block_read(V.tensor_tensor(ybuf[:, :, nb * 512:(nb + 1) * 512], G[:, b % 2, :, :],
                                           gates[:, :, nb * 512:(nb + 1) * 512], ALU.mult), "att", nb)
            dve.wait_ge(sem("ysg"), 1)
            V.tensor_tensor(yct, yct, ysg, ALU.mult).then_inc(sem("silu"), 1)
            copies("convT", [cT[:, 2 * g:2 * g + 2, :].rearrange("p c n -> p (c n)") for g in range(2)])
            split("out", 0)
            for nb in range(2):
                b = block_done(dve, "conv", nb)
                g = gates[:, :, D + nb * 512:D + (nb + 1) * 512]
                block_read(V.tensor_tensor(g, G[:, b % 2, :, :], g, ALU.mult), "conv", nb)
            for i in range(2):
                read_out(dve, "conv", i)
            for nb in range(2):
                y = ybuf[:, :, nb * 512:(nb + 1) * 512]
                V.tensor_tensor(y, y, gates[:, :, D + nb * 512:D + (nb + 1) * 512], ALU.add).then_inc(sem("mixed_c"), 1)
            turned_in("mix_c")
            split("out", 1)
            for nb in range(2):
                b = block_done(dve, "out", nb)
                x = xs[:, :, nb * 512:(nb + 1) * 512]
                block_read(V.tensor_tensor(x, x, G[:, b % 2, :, :], ALU.add), "out", nb)
            norm(5)
            dve.wait_ge(sem("l_fg"), 16)
            for t in range(TT):
                link(V.tensor_tensor(h2[:, t, :], ybuf[:, t, :], fgrow, ALU.mult))

            def top16(rows):
                start, per = n_dve[0], len(rows)
                for step in range(5):
                    for j, (vals, idx, src) in enumerate(rows):
                        if step:
                            dve.wait_ge(sem("dve_step"), start + (step - 1) * per + j + 1)
                        e = slice(8 * (step // 3), 8 * (step // 3) + 8)
                        if step in (0, 3):
                            ins = V.max(vals[:, e], src)
                        elif step in (1, 4):
                            ins = V.max_index(idx[:, e], vals[:, e], src)
                        else:
                            ins = V.match_replace(src, vals[:, 0:8], src, TAKEN)
                        ins.then_inc(sem("dve_step"), 1)
                        n_dve[0] += 1
                dve.wait_ge(sem("dve_step"), n_dve[0])

            def key_top(r0, n):
                top16([(sv[:, r // 2, r % 2, :], siu[:, r // 2, r % 2, :], psc[:, r, :]) for r in range(r0, r0 + n)])

            def pair_top(h0, n):
                top16([(topv[:, h, :], tju[:, 0, h, :], cand[:, h, :, :].rearrange("p a b -> p (a b)"))
                       for h in range(h0, h0 + n)])

            def pairs(h0=0, n=H):
                h = slice(h0, h0 + n)
                link(V.tensor_copy(sif[:, h, :, :], siu[:, h, :, :]))
                link(V.tensor_tensor(cand[:, h, :, :], bcast(sv[:, h, 0, :], 3, PK), bcast(sv[:, h, 1, :], 2, PK), ALU.add))

            def places(h0=0, n=H):
                h = slice(h0, h0 + n)
                link(V.tensor_scalar(tju[:, 1, h, :], tju[:, 0, h, :], 4, None, ALU.logical_shift_right))
                link(V.tensor_scalar(tju[:, 2, h, :], tju[:, 0, h, :], PK - 1, None, ALU.bitwise_and))
                link(V.tensor_copy(tjf[:, :, h, :], tju[:, 1:3, h, :]))

            def sub_key(c, h0=0, n=H):
                h = slice(h0, h0 + n)
                link(V.tensor_tensor(cand[:, h, :, :], bcast(tjf[:, c, h, :], 3, PK), bcast(bcast(iota16, 1, PK), 1, n),
                                     ALU.is_equal))
                link(V.tensor_tensor(eqc[:, h, :, :], cand[:, h, :, :], bcast(sif[:, h, c, :], 2, PK), ALU.mult))
                link(V.tensor_reduce(i12[:, c, h, :], eqc[:, h, :, :], AX_X, ALU.add))

            def choose(t):
                V.scalar_tensor_tensor(out=eidx[:, t, :], in0=i12[:, 0, :, :].rearrange("p h k -> p (h k)"),
                                       scalar=float(NKEYS), in1=i12[:, 1, :, :].rearrange("p h k -> p (h k)"),
                                       op0=ALU.mult, op1=ALU.add).then_inc(sem("eidx_ready"), 1)
                link(V.tensor_copy(gmax, topv[:, :, 0]))
                V.tensor_tensor(topv, topv, bcast(gmax, 2, PK), ALU.subtract).then_inc(sem("topv"), 1)
                dve.wait_ge(sem("gate_exp"), t + 1)
                link(V.tensor_reduce(gsum, topv, AX_X, ALU.add))
                link(V.reciprocal(grec, gsum))
                link(V.tensor_tensor(gateT[:, t, :].rearrange("p (h k) -> p h k", h=H), topv, bcast(grec, 2, PK), ALU.mult))

            def expert_dots(t):
                def between(i):
                    for j in range(GBUF):
                        row = gbufs[j // 4][:, j % 4, :]
                        dve.wait_ge(sem(f"row{j}"), 16 * i + 16 * (2 * t * NSEL // GBUF + 1))
                        V.scalar_tensor_tensor(out=row, in0=row, scalar=1.0, in1=h2[:, t, :], op0=ALU.mult, op1=ALU.mult,
                                               accum_out=dots[:, t, bass.ds(GBUF * i + j, 1)]).then_inc(sem("row_used"), 1)
                return between

            def expert_sums(t):
                base = (2 * t + 1) * NSEL

                def between(i):
                    for j in range(GBUF):
                        dve.wait_ge(sem(f"row{j}"), 16 * i + 16 * (base // GBUF + 1))
                        dve.wait_ge(sem("row_used"), GBUF * i + (base + j + GBUF - 1))
                        total = (xs, ybuf)[j % 2][:, t, :]
                        V.scalar_tensor_tensor(out=total, in0=gbufs[j // 4][:, j % 4, :],
                                               scalar=actv[:, t, bass.ds(GBUF * i + j, 1)],
                                               in1=total, op0=ALU.mult, op1=ALU.add).then_inc(sem("row_used"), 1)
                return between

            def peer_done(t):
                dve.wait_ge(sem("row_used"), 2 * (t + 1) * NSEL + GBUF)
                V.tensor_tensor(xs[:, t, :], xs[:, t, :], ybuf[:, t, :], ALU.add).then_inc(sem("x_ready"), 1)

            def weights_of(t):
                dve.wait_ge(sem("row_used"), (2 * t + 1) * NSEL + GBUF)
                V.memset(gmax, 0.0).then_inc(sem("dots_all"), 1)
                dve.wait_ge(sem("gelu"), t + 1)
                V.memset(ybuf[:, t, :], 0.0).then_inc(sem("sum_zeroed"), 1)
                dve.wait_ge(sem("sum_zeroed"), t + 1)
                link(V.tensor_tensor(actv[:, t, :], actv[:, t, :], gateT[:, t, :], ALU.mult))

            def experts(uses, i0, i1):
                with dve.Fori(i0, i1) as i:
                    uses(i)

            rounds = NSEL // GBUF
            for i in range(2):
                dve.wait_ge(m_free, SPARE0["psc"] + i + 1)
                key_top(H * i, 4)
                key_top(H * i + 4, 4)
                pairs(4 * i, 4)
                pair_top(4 * i, 4)
                places(4 * i, 4)
                sub_key(0, 4 * i, 4)
                sub_key(1, 4 * i, 4)
            choose(0)
            dve.wait_ge(m_free, SPARE0["psc"] + 4)
            for r0 in range(0, HC, 2):
                key_top(r0, 2)
                experts(expert_dots(0), r0 * rounds // HC, (r0 + 2) * rounds // HC)
            weights_of(0)
            experts(expert_sums(0), 0, 1)
            pairs()
            for h0 in range(0, H, 2):
                experts(expert_sums(0), h0 + 1, h0 + 3)
                pair_top(h0, 2)
            experts(expert_sums(0), H + 1, H + 3)
            places()
            sub_key(0)
            experts(expert_sums(0), H + 3, H + 5)
            sub_key(1)
            choose(1)
            experts(expert_sums(0), H + 5, rounds)
            peer_done(0)

            def embed_norm(t):
                dve.wait_ge(sem("norm_std"), 7 + t)
                V.reciprocal(rstd[:, t:t + 1], std[:, t:t + 1]).then_inc(sem("norm_rstd"), 1)

            def embed_turned(t):
                for g in range(2):
                    p = turn_done("norm6", 2 * t + g)
                    c = slice(4 * g, 4 * g + 4)
                    V.tensor_tensor(hT[:, c, t * P:(t + 1) * P], T[:, p, :].rearrange("p (c n) -> p c n", c=4),
                                    bcast(ncols[:, 6, c], 2, P), ALU.mult).then_inc(t_free[p], 1)

            def embed_add(t):
                b = block_done(dve, "ple", 2 * t)
                read_out(dve, "ple", 2 * t + 1)
                g = sig[:, t, :].rearrange("p (a n) -> p a n", a=2)
                block_read(V.tensor_tensor(g, G[:, b % 2, :, :], g, ALU.mult), "ple", 2 * t)
                read_out(dve, "ple", 2 * t)
                V.tensor_tensor(xs[:, t, :], xs[:, t, :], sig[:, t, :], ALU.add).then_inc(sem("out_done"), 1)

            experts(expert_dots(1), 0, 2)
            embed_norm(0)
            experts(expert_dots(1), 2, 4)
            embed_turned(0)
            experts(expert_dots(1), 4, 8)
            embed_add(0)
            experts(expert_dots(1), 8, rounds)
            weights_of(1)
            experts(expert_sums(1), 0, rounds)
            peer_done(1)
            embed_norm(1)
            embed_turned(1)
            embed_add(1)


def kernel(**inputs):
    import numpy as np
    import concourse.bacc as bacc
    from concourse.bass_utils import run_bass_kernel_spmd

    v = {k: np.asarray(a) for k, a in inputs.items()}

    def chunks(w):
        return w.reshape(-1, P, w.shape[1]).transpose(1, 0, 2).reshape(P, -1)

    def col(a):
        return np.ascontiguousarray(np.moveaxis(a.reshape(a.shape[:-1] + (-1, P)), -1, 0))

    def by_cols(w, c0, n):
        return [w[:, c0 + 256 * i:c0 + 256 * (i + 1)] for i in range(2 * n)]

    def down(w):
        return [w[D * g:D * (g + 1), 256 * i:256 * (i + 1)] for i in range(4) for g in range(w.shape[0] // D)]

    wa, wb, wc = v["a_w_in"][0], v["b_w_in"][0], v["w_in_2"][0]
    ada = {name: by_cols(v["ada_w"][l], 512 * first, dict(UNITS)[name]) for name, (l, first) in ADA.items()}
    weights = {
        **ada, "a_qk": by_cols(wa, 0, 2), "a_v": by_cols(wa, 1024, 2), "a_o": by_cols(wa, 2048, 2),
        "a_out": by_cols(v["a_w_out"][0], 0, 2),
        "up0": by_cols(v["ffn_w1"][0], 0, 8), "down0": down(v["ffn_w2"][0]),
        "up1": by_cols(v["ffn_w1"][1], 0, 8), "down1": down(v["ffn_w2"][1]),
        "b_u": by_cols(wb, 0, 4), "b_v": by_cols(wb, GH, 4), "b_out": down(v["b_w_out"][0]),
        "qkv": by_cols(wc, 0, 3), "qi": by_cols(wc, 1536, 1), "glu": by_cols(wc, 2120, 2),
        "gates": by_cols(wc, 3144, 4), "att": np.split(v["w_att_out_2"][0], 2, axis=1),
        "conv": np.split(v["w_conv_out_2"][0], 2, axis=1),
        "out": by_cols(v["w_out_2"][0], 0, 2), "peer_q": TT * by_cols(v["w_peer_q_2"][0], 0, 4),
        "ple": by_cols(v["w_ple_gate_2"][0], 0, 2),
    }
    ki, wi = wc[:, 2048:2112], wc[:, 2112:2120]

    p = np.arange(P)
    seen = [np.where(np.arange(P * (t + 1))[None, :] // 64 <= (P * t + p[:, None]) // 64, 0.0, NEG) for t in range(TT)]
    consts = np.concatenate([
        np.eye(P), p[:, None] <= p[None, :], np.where(p[None, :] <= p[:, None], 0.0, NEG),
        p[:, None] + p[None, :] == P - 1, *seen, np.tile(np.arange(16), (P, 1))], axis=1).astype(np.float32)
    rel = np.arange(RELS) - 255
    far = 8 + (np.log(np.maximum(np.abs(rel), 1) / 8) / np.log(1024 / 8) * 8).astype(np.int32)
    bucket = np.where(rel > 0, 16, 0) + np.where(np.abs(rel) < 8, np.abs(rel), np.minimum(far, 15))
    onehot = (np.arange(32)[:, None] == bucket[None, :]).astype(np.float32)

    given = {
        "wpack": np.stack([chunks(w) for name, _ in UNITS for w in weights[name]]),
        "x": v["x"][0], "c": col(v["c"][0]), "norm_g": v["norm_g"],
        "ncols": col(np.stack([v["norm_g"][0, 0], v["norm_g"][0, 2], v["norm_g"][1, 0], v["norm_g"][1, 2],
                               v["attn_norm_g_2"][0], v["ffn_norm_g_2"][0], v["ple_norm_g_2"][0]])),
        "ada_b": v["ada_b"], "wgate": chunks(wa[:, 3072:3088]).reshape(P, DC, 16), "b_if": v["a_b_if"][0],
        "hnorm_g": v["a_hnorm_g"][0], "bu": col(v["b_b_in"][0, :GH]), "bv": v["b_b_in"][0, GH:],
        "ln_g": v["b_ln_g"][0], "ln_b": v["b_ln_b"][0], "wsT": v["b_ws"][0].transpose(2, 0, 1),
        "bs": v["b_bs"][0].reshape(-1), "rel_bias": v["rel_bias_2"], "onehot": onehot, "consts": consts,
        "wkiwi": chunks(np.concatenate([ki, ki, wi], axis=1)).reshape(P, DC, 2 * AH + H),
        "b_gate": v["b_gate_2"][0], "q_norm_g": v["q_norm_g_2"][0], "k_norm_g": v["k_norm_g_2"][0],
        "conv_w": np.moveaxis(v["conv_w_2"][0, :, 0, :].reshape(TAPS, CH // P, P), (2, 1, 0), (0, 1, 2)),
        "conv_b": col(v["conv_b_2"][0]), "conv_ln_g": v["conv_ln_g_2"][0], "conv_ln_b": v["conv_ln_b_2"][0],
        "ffn_norm_g": v["ffn_norm_g_2"][0],
        "skT": v["peer_sub_keys_2"][0].reshape(HC, NKEYS, P).transpose(2, 0, 1),
        "peer_u": v["peer_u_2"][0], "peer_v": v["peer_v_2"][0],
        "pT": v["p_2"][0, 0].T.reshape(2, P, TOK).transpose(1, 0, 2),
        "w_ple_proj": v["w_ple_proj_2"][0].reshape(2, P, D).transpose(1, 0, 2),
    }
    given = {k: np.ascontiguousarray(a) for k, a in given.items()}
    nc = bacc.Bacc("TRN2", target_bir_lowering=False, num_devices=1)
    A = {k: nc.dram_tensor(f"in_{k}", a.shape, F32, kind="ExternalInput").ap() for k, a in given.items()}
    out = nc.dram_tensor("out", (TOK, D), F32, kind="ExternalOutput").ap()
    build(nc, A, out)
    r = run_bass_kernel_spmd(nc, [{f"in_{k}": a for k, a in given.items()}], core_ids=[0])
    return r.results[0]["out"].reshape(1, TOK, D)
```
